# Optimizing a Trainium2 kernel written in Bass

```python
import math
import jax, jax.numpy as jnp
from jax import lax
import numpy as np

D_MODEL = 1024
BATCH = 1
SEQ = 256
DEPTH = 1
DEC_BATCH = 8
DEC_SEQ = 1
PAST_LEN = 2048
PAGE_SIZE = 128

C_CONF = D_MODEL
CONF_GROUPS = 16
K_CONF = 31
D_INNER = D_MODEL
SSM_HEAD_DIM = 64
N_SSM_HEADS = D_INNER // SSM_HEAD_DIM
N_SSM_GROUPS = 4
D_STATE = 128
K_SSM = 4
CHUNK = 128
CONV_DIM = D_INNER + 2 * N_SSM_GROUPS * D_STATE
D_MIX = C_CONF + D_INNER
IN_COLS = 2 * C_CONF + D_INNER + CONV_DIM + N_SSM_HEADS
N_EXPERT_GROUPS = 4
EXPERTS_PER_GROUP = 4
N_EXPERTS = N_EXPERT_GROUPS * EXPERTS_PER_GROUP
TOP_K = 2
D_FF_EXPERT = D_MODEL // 2
PLE_DIM = 256
EPS = 1e-6

kernel_name = 'hybrid_conv_ssd_hmoe_step'

def rmsnorm(x, g):
    xf = x.astype(jnp.float32)
    xf = xf * lax.rsqrt(jnp.mean(xf * xf, axis=-1, keepdims=True) + EPS)
    return (xf * g.astype(jnp.float32)).astype(x.dtype)

def layernorm(x, g, b):
    xf = x.astype(jnp.float32)
    xc = xf - jnp.mean(xf, axis=-1, keepdims=True)
    var = jnp.mean(xc * xc, axis=-1, keepdims=True)
    return (xc * lax.rsqrt(var + EPS) * g.astype(jnp.float32) + b.astype(jnp.float32)).astype(x.dtype)

def causal_dwconv(u, buf, w, b):
    k = w.shape[0]
    full = jnp.concatenate([buf.astype(u.dtype), u], axis=1)
    out = lax.conv_general_dilated(full, w.astype(u.dtype)[:, None, :], window_strides=(1,),
                                   padding='VALID', dimension_numbers=('NWC', 'WIO', 'NWC'),
                                   feature_group_count=u.shape[-1])
    return out + b.astype(u.dtype), full[:, full.shape[1] - (k - 1):]

def segsum(a):
    q = a.shape[-1]
    cs = jnp.cumsum(a, axis=-1)
    diff = cs[..., :, None] - cs[..., None, :]
    return jnp.where(jnp.tril(jnp.ones((q, q), dtype=bool)), diff, -jnp.inf)

def ssd_scan(xs, dt, a_neg, bm, cm, h0):
    bsz, L, H, P = xs.shape
    G, N = bm.shape[2], bm.shape[3]
    R = H // G
    q = min(CHUNK, L)
    n_chunks = -(-L // q)
    pad = n_chunks * q - L
    padw = lambda t: jnp.pad(t, [(0, 0), (0, pad)] + [(0, 0)] * (t.ndim - 2))
    x = padw(xs).reshape(bsz, n_chunks, q, G, R, P)
    d = padw(dt).reshape(bsz, n_chunks, q, G, R)
    bb = padw(bm).reshape(bsz, n_chunks, q, G, N)
    cc = padw(cm).reshape(bsz, n_chunks, q, G, N)
    at = jnp.moveaxis(d * a_neg.reshape(G, R), 2, -1)
    acs = jnp.cumsum(at, axis=-1)
    lmat = jnp.exp(segsum(at))
    xdt = x * d[..., None]
    cb = jnp.einsum('bclgn,bcsgn->bcgls', cc, bb)
    y_diag = jnp.einsum('bcgls,bcgrls,bcsgrp->bclgrp', cb, lmat, xdt)
    decay_states = jnp.exp(acs[..., -1:] - acs)
    states = jnp.einsum('bclgn,bcgrl,bclgrp->bcgrpn', bb, decay_states, xdt)
    chunk_decay = jnp.exp(acs[..., -1])

    def step(h, inp):
        dec, st = inp
        return dec[..., None, None] * h + st, h

    h_last, h_prev = lax.scan(step, h0.reshape(bsz, G, R, P, N),
                              (jnp.moveaxis(chunk_decay, 1, 0), jnp.moveaxis(states, 1, 0)))
    h_prev = jnp.moveaxis(h_prev, 0, 1)
    y_off = jnp.einsum('bclgn,bcgrpn,bcgrl->bclgrp', cc, h_prev, jnp.exp(acs))
    y = (y_diag + y_off).reshape(bsz, n_chunks * q, H, P)[:, :L]
    return y, h_last.reshape(bsz, H, P, N)

def mixer_block(u, cbuf, mbuf, sh, w_in, conf_dw_w, conf_dw_b, conf_ln_g, conf_ln_b,
                ssm_conv_w, ssm_conv_b, dt_bias, a_log, d_skip, ssm_norm_g, w_out):
    bsz, L, _ = u.shape
    proj = u @ w_in
    o1 = 2 * C_CONF
    o2 = o1 + D_INNER
    o3 = o2 + CONV_DIM
    glu = proj[..., :C_CONF] * jax.nn.sigmoid(proj[..., C_CONF:o1])
    cconv, new_cbuf = causal_dwconv(glu, cbuf, conf_dw_w, conf_dw_b)
    a_out = jax.nn.silu(layernorm(cconv, conf_ln_g, conf_ln_b))
    z = proj[..., o1:o2]
    xbc, new_mbuf = causal_dwconv(proj[..., o2:o3], mbuf, ssm_conv_w, ssm_conv_b)
    xbc = jax.nn.silu(xbc).astype(jnp.float32)
    gn = N_SSM_GROUPS * D_STATE
    xs = xbc[..., :D_INNER].reshape(bsz, L, N_SSM_HEADS, SSM_HEAD_DIM)
    bm = xbc[..., D_INNER:D_INNER + gn].reshape(bsz, L, N_SSM_GROUPS, D_STATE)
    cm = xbc[..., D_INNER + gn:].reshape(bsz, L, N_SSM_GROUPS, D_STATE)
    dt = jax.nn.softplus(proj[..., o3:].astype(jnp.float32) + dt_bias.astype(jnp.float32))
    a_neg = -jnp.exp(a_log.astype(jnp.float32))
    y, new_sh = ssd_scan(xs, dt, a_neg, bm, cm, sh.astype(jnp.float32))
    y = y + d_skip.astype(jnp.float32)[:, None] * xs
    y = y.reshape(bsz, L, D_INNER).astype(u.dtype) * jax.nn.silu(z)
    m_out = rmsnorm(y.reshape(bsz, L, N_SSM_GROUPS, D_INNER // N_SSM_GROUPS),
                    ssm_norm_g.reshape(N_SSM_GROUPS, D_INNER // N_SSM_GROUPS)).reshape(bsz, L, D_INNER)
    out = jnp.concatenate([a_out, m_out], axis=-1) @ w_out
    return out, new_cbuf, new_mbuf, new_sh.astype(sh.dtype)

def hier_moe(u, w_rg, b_rg, w_re, b_re, w_gate_e, w_up_e, w_down_e):
    shp = u.shape
    t = u.reshape(-1, shp[-1])
    p_grp = jax.nn.softmax((t @ w_rg + b_rg).astype(jnp.float32), axis=-1)
    g_val, g_idx = lax.top_k(p_grp, 1)
    le = (t @ w_re + b_re).astype(jnp.float32).reshape(-1, N_EXPERT_GROUPS, EXPERTS_PER_GROUP)
    sel = jax.nn.one_hot(g_idx[:, 0], N_EXPERT_GROUPS, dtype=jnp.float32)
    le_sel = jnp.einsum('tge,tg->te', le, sel)
    e_val, e_idx = lax.top_k(jax.nn.softmax(le_sel, axis=-1), TOP_K)
    wts = g_val * e_val / jnp.sum(e_val, axis=-1, keepdims=True)
    eid = g_idx * EXPERTS_PER_GROUP + e_idx
    combine = jnp.sum(jax.nn.one_hot(eid, N_EXPERTS, dtype=jnp.float32) * wts[..., None], axis=1).astype(u.dtype)
    out = jnp.zeros_like(t)
    for e in range(N_EXPERTS):
        hdn = jax.nn.silu(t @ w_gate_e[e]) * (t @ w_up_e[e])
        out = out + combine[:, e:e + 1] * (hdn @ w_down_e[e])
    return out.reshape(shp)

def layer(h, p, cbuf, mbuf, sh, g_mix, w_in, conf_dw_w, conf_dw_b, conf_ln_g, conf_ln_b,
          ssm_conv_w, ssm_conv_b, dt_bias, a_log, d_skip, ssm_norm_g, w_out, g_ffn,
          w_rg, b_rg, w_re, b_re, w_gate_e, w_up_e, w_down_e, g_ple, w_ple_gate, w_ple):
    mix, cbuf, mbuf, sh = mixer_block(rmsnorm(h, g_mix), cbuf, mbuf, sh, w_in, conf_dw_w, conf_dw_b,
                                      conf_ln_g, conf_ln_b, ssm_conv_w, ssm_conv_b, dt_bias, a_log,
                                      d_skip, ssm_norm_g, w_out)
    h = h + mix
    h = h + hier_moe(rmsnorm(h, g_ffn), w_rg, b_rg, w_re, b_re, w_gate_e, w_up_e, w_down_e)
    h = h + (p.astype(h.dtype) @ w_ple) * jax.nn.sigmoid(rmsnorm(h, g_ple) @ w_ple_gate)
    return h, cbuf, mbuf, sh

def setup_inputs(seed: int = 0) -> dict:
    key = jax.random.key(seed)
    ks = iter(jax.random.split(key, 48))
    f32 = jnp.float32

    def nrm(shape, scale):
        return jax.random.normal(next(ks), shape, f32) * scale

    def gain(shape):
        return 1.0 + 0.05 * jax.random.normal(next(ks), shape, f32)

    dt0 = jnp.exp(jax.random.uniform(next(ks), (DEPTH, N_SSM_HEADS), f32,
                                     minval=math.log(1e-3), maxval=math.log(1e-1)))
    dt_bias = dt0 + jnp.log(-jnp.expm1(-dt0))
    a_log = jnp.log(jax.random.uniform(next(ks), (DEPTH, N_SSM_HEADS), f32, minval=1.0, maxval=16.0))
    return {
        'x_prompt': nrm((BATCH, SEQ, D_MODEL), 1.0),
        'x_sample': nrm((DEC_BATCH, DEC_SEQ, D_MODEL), 1.0),
        'p_prompt': nrm((DEPTH, BATCH, SEQ, PLE_DIM), 1.0),
        'p_sample': nrm((DEPTH, DEC_BATCH, DEC_SEQ, PLE_DIM), 1.0),
        'state_conf_conv': nrm((DEPTH, DEC_BATCH, K_CONF - 1, C_CONF), 0.5),
        'state_ssm_conv': nrm((DEPTH, DEC_BATCH, K_SSM - 1, CONV_DIM), 1.0),
        'state_ssm': nrm((DEPTH, DEC_BATCH, N_SSM_HEADS, SSM_HEAD_DIM, D_STATE), 0.3),
        'g_mix': gain((DEPTH, D_MODEL)),
        'w_in': nrm((DEPTH, D_MODEL, IN_COLS), D_MODEL ** -0.5),
        'conf_dw_w': nrm((DEPTH, K_CONF, C_CONF), K_CONF ** -0.5),
        'conf_dw_b': nrm((DEPTH, C_CONF), 0.02),
        'conf_ln_g': gain((DEPTH, C_CONF)),
        'conf_ln_b': nrm((DEPTH, C_CONF), 0.02),
        'ssm_conv_w': nrm((DEPTH, K_SSM, CONV_DIM), K_SSM ** -0.5),
        'ssm_conv_b': nrm((DEPTH, CONV_DIM), 0.02),
        'dt_bias': dt_bias,
        'a_log': a_log,
        'd_skip': gain((DEPTH, N_SSM_HEADS)),
        'ssm_norm_g': gain((DEPTH, D_INNER)),
        'w_out': nrm((DEPTH, D_MIX, D_MODEL), D_MIX ** -0.5),
        'g_ffn': gain((DEPTH, D_MODEL)),
        'w_rg': nrm((DEPTH, D_MODEL, N_EXPERT_GROUPS), D_MODEL ** -0.5),
        'b_rg': nrm((DEPTH, N_EXPERT_GROUPS), 0.01),
        'w_re': nrm((DEPTH, D_MODEL, N_EXPERTS), D_MODEL ** -0.5),
        'b_re': nrm((DEPTH, N_EXPERTS), 0.01),
        'w_gate_e': nrm((DEPTH, N_EXPERTS, D_MODEL, D_FF_EXPERT), D_MODEL ** -0.5),
        'w_up_e': nrm((DEPTH, N_EXPERTS, D_MODEL, D_FF_EXPERT), D_MODEL ** -0.5),
        'w_down_e': nrm((DEPTH, N_EXPERTS, D_FF_EXPERT, D_MODEL), D_FF_EXPERT ** -0.5),
        'g_ple': gain((DEPTH, D_MODEL)),
        'w_ple_gate': nrm((DEPTH, D_MODEL, D_MODEL), D_MODEL ** -0.5),
        'w_ple': nrm((DEPTH, PLE_DIM, D_MODEL), PLE_DIM ** -0.5),
        'g_final': gain((D_MODEL,)),
    }

def reference(x_prompt, x_sample, p_prompt, p_sample, state_conf_conv, state_ssm_conv, state_ssm,
              g_mix, w_in, conf_dw_w, conf_dw_b, conf_ln_g, conf_ln_b, ssm_conv_w, ssm_conv_b,
              dt_bias, a_log, d_skip, ssm_norm_g, w_out, g_ffn, w_rg, b_rg, w_re, b_re,
              w_gate_e, w_up_e, w_down_e, g_ple, w_ple_gate, w_ple, g_final):
    hp, hs = x_prompt, x_sample
    bp = x_prompt.shape[0]
    cp_l, mp_l, sp_l, cs_l, ms_l, ss_l = [], [], [], [], [], []
    for i in range(DEPTH):
        lw = (g_mix[i], w_in[i], conf_dw_w[i], conf_dw_b[i], conf_ln_g[i], conf_ln_b[i],
              ssm_conv_w[i], ssm_conv_b[i], dt_bias[i], a_log[i], d_skip[i], ssm_norm_g[i], w_out[i],
              g_ffn[i], w_rg[i], b_rg[i], w_re[i], b_re[i], w_gate_e[i], w_up_e[i], w_down_e[i],
              g_ple[i], w_ple_gate[i], w_ple[i])
        hp, c, m, s = layer(hp, p_prompt[i],
                            jnp.zeros((bp, K_CONF - 1, C_CONF), hp.dtype),
                            jnp.zeros((bp, K_SSM - 1, CONV_DIM), hp.dtype),
                            jnp.zeros((bp, N_SSM_HEADS, SSM_HEAD_DIM, D_STATE), jnp.float32), *lw)
        cp_l.append(c)
        mp_l.append(m)
        sp_l.append(s)
        hs, c, m, s = layer(hs, p_sample[i], state_conf_conv[i], state_ssm_conv[i], state_ssm[i], *lw)
        cs_l.append(c)
        ms_l.append(m)
        ss_l.append(s)
    y_prompt = rmsnorm(hp, g_final)
    y_sample = rmsnorm(hs, g_final)
    return (y_prompt, y_sample, jnp.stack(cp_l), jnp.stack(mp_l), jnp.stack(sp_l),
            jnp.stack(cs_l), jnp.stack(ms_l), jnp.stack(ss_l))


_drawn_inputs = setup_inputs


def setup_inputs(seed=0):
    import zlib

    import numpy as np

    out = dict(_drawn_inputs(seed))
    spreads = {}
    factors = {'conf_dw_b': 2.785,
     'conf_ln_b': 4.069,
     'd_skip': 2.8,
     'b_rg': 4.311,
     'b_re': 6.383,
     'g_ple': 7.336}
    for name, (base, spread) in spreads.items():
        noise = np.random.default_rng([zlib.crc32(name.encode()), seed]).standard_normal(out[name].shape)
        drawn = base * np.exp(spread * noise) if base else spread * noise
        out[name] = __import__('jax').numpy.asarray(drawn.astype(out[name].dtype))
    for name, factor in factors.items():
        out[name] = (out[name] * factor).astype(out[name].dtype)
    return out
```

```python
from contextlib import ExitStack

import numpy as np

import concourse.bass as bass
from concourse import mybir

ALU = mybir.AluOpType
ACT = mybir.ActivationFunctionType
AX = mybir.AxisListType
F32 = mybir.dt.float32
I32 = mybir.dt.int32

P = 128
D = 1024
KD = D // P
NPR = 256
NSM = 8
T = NPR + NSM
KC = 31
KS = 4
NH = 16
HD = 64
NG = 4
NX = 16
Q = 128
NE = 16
CAP = 64
MAXQ = -(-T // CAP)
PAIRS = NE // 2
FF = 512
EPS = 1e-6
SLOT = 2048
MIXR = 4
MOER = 12
NWIN = 20
NWOUT = 8
MOE_SLOT = [8, 4, 5, 6, 7, 9, 10, 11, 0, 1, 2, 3]
W_IN_ORDER = [(kind, i) for g in range(4) for kind, i in (("g", g), ("x", 2 * g), ("x", 2 * g + 1))] + \
             [("g", g) for g in range(4, 8)] + [("z", i) for i in range(4)]
NEARLY = 12
SLOT_AFTER = {0: 14, 2: 15, 4: 16, 5: 17, 6: 18, 7: 19}
AT = {ki: n for n, ki in enumerate(W_IN_ORDER)}
TOK = [(0, 128), (128, 128), (256, 8)]

PRM = {}
_at = 0
for _n, _w in (("g_mix", 8), ("conv_b", 8), ("ln_g", 8), ("ln_b", 8), ("ssm_g", 8), ("g_ffn", 8), ("g_ple", 8),
               ("g_final", 8), ("d_skip", 8), ("xconv_b", 16), ("conv_w", 8 * KC), ("xconv_w", 16 * KS)):
    PRM[_n] = (_at, _w)
    _at += _w
NPRM = _at


def build(nc, xT, pT, w_in, w_dt, w_out, w_moe, w_router, b_router, w_pleg, w_ple, params, hparams,
          conf_s, ssm_s, state_s, yT, conf_p_out, ssm_p_out, h_p_out, conf_s_out, ssm_s_out, h_s_out):
    with ExitStack() as ctx:
        def sb(name, shape, dt=F32):
            return ctx.enter_context(nc.sbuf_tensor(name, shape, dt))

        def sem(name):
            return ctx.enter_context(nc.semaphore(name))

        ring = sb("ring", [P, MOER, SLOT])
        h = sb("h", [P, KD, T])
        u = sb("u", [P, KD, T])
        prm = sb("prm", [P, NPRM])
        ident = sb("ident", [P, P])
        mean_k = sb("mean_k", [P, P])
        mean_g = sb("mean_g", [P, P])
        causal = sb("causal", [P, P])[:, :]
        eps = sb("eps", [P, 1])
        glu = sb("glu", [P, KD, KC - 1 + NPR])
        cat = sb("cat", [P, 2 * KD, T])
        xraw = sb("xraw", [P, NX, KS - 1 + NPR])
        xraw_s = sb("xraw_s", [P, NX, KS, NSM])
        xbc = sb("xbc", [P, NX, T])
        btok = sb("btok", [P, 2, NG, P])
        hst = sb("hst", [P, D])
        cbm = sb("cbm", [P, 2, NG, P])
        mexp = sb("mexp", [P, 2, 4, P])
        ea = sb("ea", [P, 4, P])
        prod = sb("prod", [P, 256])
        asg = sb("asg", [P, 2, 2, T])
        lnv = asg[:, :, :, :].rearrange("p a b n -> p (a b) n")
        cdec = sb("cdec", [P, 4])
        hp = sb("hp", [NH, 2])
        hs = sb("hs", [NH, 6, T])
        htok = sb("htok", [P, 6, NH])
        chd = sb("chd", [P, KD, 16])
        dtx = sb("dtx", [P, KD, NSM])
        wdt = sb("wdt", [P, KD, NH])
        scratch = ring[:, MIXR:MOER, :].rearrange("p a b -> p (a b)")
        state = scratch[:, 0:8192].rearrange("p (j b n) -> p j b n", j=KD, b=NSM)
        outer = scratch[:, 8192:10240].rearrange("p (q b n) -> p q b n", q=2, b=NSM)
        glu_s = scratch[:, 10240:12224].rearrange("p (j k b) -> p j k b", j=KD, k=KC)
        zs = scratch[:, 12224:12224 + KD * T].rearrange("p (j n) -> p j n", j=KD)
        cbc = scratch[:, 14336:16384].rearrange("p (q b n) -> p q b n", q=2, b=NSM)
        x0 = xraw[:, :, :].rearrange("p a b -> p (a b)")
        xdt = x0[:, 0:2 * D].rearrange("p (c n) -> p c n", c=2)
        xdec = x0[:, 2 * D:4 * D].rearrange("p (c n) -> p c n", c=2)
        a0 = xbc[:, :, :].rearrange("p a b -> p (a b)")
        utok = a0[:, 0:3 * D].rearrange("p (t n) -> p t n", t=3)
        sel = a0[:, 3072:3456].rearrange("p (t n) -> p t n", t=3)
        selw = a0[:, 3456:3840].rearrange("p (t n) -> p t n", t=3)
        xg = x0[:, 0:1024].rearrange("p (c n) -> p c n", c=KD)
        ysb = x0[:, 1024:2048].rearrange("p (c n) -> p c n", c=KD)
        silu_e = x0[:, 2048:2560]
        hid = x0[:, 2560:3072]
        hidt = x0[:, 3072:3584].rearrange("p (k n) -> p k n", k=4)
        c0 = glu[:, :, :].rearrange("p a b -> p (a b)")
        selt = c0[:, 0:T]
        seltmp = c0[:, 384:768].rearrange("p (t n) -> p t n", t=3)
        iota_s = c0[:, 768:896]
        before = c0[:, 896:1024]
        ones = c0[:, 1024:1152]
        r0 = mexp[:, :, :, :].rearrange("p a b c -> p (a b c)")

        def small(at, n):
            return r0[:, at:at + 3 * n].rearrange("p (t n) -> p t n", t=3)

        logit = small(0, 20)
        gmax, gsum, gval, gmin, m1, m2, n1, n2, e2, w1, w2, gs1, gs2, q1, q2, ps1, ps2, t1 = [
            small(60 + 3 * i, 1) for i in range(18)]
        gd, gexp, gc, gsel, le, ld, lc, oh1, le2, lc2, oh2 = [small(120 + 12 * i, 4) for i in range(11)]
        prod16, a1, a2, a12, pos = [small(260 + 48 * i, 16) for i in range(5)]
        wr = c0[:, 1152:1312].rearrange("p (k n) -> p k n", k=KD)
        br = c0[:, 1312:1332]
        tot = r0[:, 510:526]
        mc = r0[:, 526:527]
        nr = r0[:, 527:528]
        iota4 = r0[:, 528:532]
        nsteps = sb("nsteps", [P, 2], I32)
        pt = cat[:, 8:10, :]
        sg = cat[:, 10:12, :]
        yo = cat[:, 0:8, :]

        ps = ctx.enter_context(nc.psum_tensor("ps", [P, 8, 512], F32))
        XT = [2, 3, 5, 6]
        BC = [4, 7]
        SC = [7, 2]

        def par(name, i=0, n=None):
            a, w = PRM[name]
            return prm[:, a + i:a + i + (1 if n is None else n)]

        in_x, in_prm, in_h, in_dt, in_cs, in_ss, in_st, in_wr, in_p = [sem("in_" + n) for n in
            ("x", "prm", "hparams", "wdt", "conf_s", "ssm_s", "state", "router", "ple")]
        consts = sem("consts")
        mix_loaded = [sem(f"mix_loaded{i}") for i in range(MIXR)]
        sq_ready = sem("sq_ready")
        stat_ready = sem("stat_ready")
        rs_ready = sem("rs_ready")
        u_ready = sem("u_ready")
        proj_ready = sem("proj_ready")
        proj_evac = sem("proj_evac")
        glu_ready = sem("glu_ready")
        dt_ready = sem("dt_ready")
        act_self = sem("act_self")
        dve_self = sem("dve_self")
        pool_self = sem("pool_self")
        conv_done = sem("conv_done")
        conv_s_done = sem("conv_s_done")
        xconv_done = sem("xconv_done")
        xbc_ready = sem("xbc_ready")
        ln_mean = sem("ln_mean")
        ln_xc = sem("ln_xc")
        ln_sq = sem("ln_sq")
        ln_var = sem("ln_var")
        ln_rs = sem("ln_rs")
        ln_n = sem("ln_n")
        a_out_ready = sem("a_out_ready")
        dt_act = sem("dt_act")
        dt_dve = sem("dt_dve")
        hrow_ready = sem("hrow_ready")
        htok_psum = sem("htok_psum")
        htok_ready = sem("htok_ready")
        xtok_psum = sem("xtok_psum")
        xtok_ready = sem("xtok_ready")
        btok_psum = sem("btok_psum")
        btok_ready = sem("btok_ready")
        cb_psum = sem("cb_psum")
        cb_ready = sem("cb_ready")
        bc_psum = sem("bc_psum")
        dif_ready = sem("dif_ready")
        exp_ready = sem("exp_ready")
        ea_ready = sem("ea_ready")
        m_ready = sem("m_ready")
        ce_ready = sem("ce_ready")
        y_psum = sem("y_psum")
        st_ready = sem("st_ready")
        y_ready = sem("y_ready")
        hp_done = sem("hp_done")
        dtx_ready = sem("dtx_ready")
        bbc_psum = sem("bbc_psum")
        cbc_psum = sem("cbc_psum")
        cbc_ready = sem("cbc_ready")
        outer_ready = sem("outer_ready")
        snew_ready = sem("snew_ready")
        ttr_done = sem("ttr_done")
        y_s_ready = sem("y_s_ready")
        ycat_ready = sem("ycat_ready")
        gsq_ready = sem("gsq_ready")
        gstat = sem("gstat")
        grs = sem("grs")
        m_out_ready = sem("m_out_ready")
        o_psum = sem("o_psum")
        o_added = sem("o_added")
        out_conf_p, out_ssm_p, out_h_p, out_conf_s, out_ssm_s, out_h_s, out_y = [sem("out_" + n) for n in
            ("conf_p", "ssm_p", "h_p", "conf_s", "ssm_s", "h_s", "y")]
        log_psum = sem("log_psum")
        utok_psum = sem("utok_psum")
        utok_ready = sem("utok_ready")
        r_dve = sem("r_dve")
        r_act = sem("r_act")
        assigned = sem("assigned")
        pos_psum = sem("pos_psum")
        routes = sem("routes")
        sel_ready = sem("sel_ready")
        selw_ready = sem("selw_ready")
        xg_psum = sem("xg_psum")
        xg_ready = sem("xg_ready")
        moe_loaded = [sem(f"moe_loaded{i}") for i in range(MOER)]
        moe_used = [sem(f"moe_used{i}") for i in range(MOER)]
        gate_done, up_done, down_done = moe_used[3], moe_used[7], moe_used[11]
        silu_ready = sem("silu_ready")
        hid_ready = sem("hid_ready")
        hidt_psum = sem("hidt_psum")
        hidt_ready = sem("hidt_ready")
        selt_psum = sem("selt_psum")
        selt_ready = sem("selt_ready")
        ytok_ready = sem("ytok_ready")
        sc_psum = [sem(f"sc_psum{q}") for q in range(2)]
        sc_added = [sem(f"sc_added{q}") for q in range(2)]
        selw_parts = sem("selw_parts")
        gs_moved = sem("gs_moved")
        sel_half = sem("sel_half")
        ple_loaded = sem("ple_loaded")
        gate_psum = sem("gate_psum")
        gate_sig = sem("gate_sig")
        gate_mul = sem("gate_mul")
        h_ple = sem("h_ple")
        yo_ready = sem("yo_ready")

        block = ctx.enter_context(nc.Block())

        @block.sync
        def _(sp):
            def read(n):
                if n < NWIN:
                    sp.wait_ge(proj_ready, 2 * n + 2)
                else:
                    sp.wait_ge(o_psum, n - NWIN + 1)

            for n in range(NWIN + NWOUT):
                if n >= MIXR:
                    read(n - MIXR)
                src = w_in[n] if n < NWIN else w_out[n - NWIN]
                sp.dma_start(ring[:, n % MIXR, :], src).then_inc(mix_loaded[n % MIXR], 16)
            last_user = {n % MIXR: n for n in range(NWIN + NWOUT)}
            for j in range(MOER):
                s = MOE_SLOT[j]
                if s < MIXR:
                    read(last_user[s])
                elif s >= 9:
                    sp.wait_ge(ycat_ready, 1)
                    sp.wait_ge(out_conf_s, 16)
                    sp.wait_ge(y_s_ready, KD)
                elif s == 8:
                    sp.wait_ge(snew_ready, KD)
                else:
                    sp.wait_ge(out_h_s, 16 * KD)
                    sp.wait_ge(y_s_ready, KD)
                sp.dma_start(ring[:, s, :], w_moe[0, j]).then_inc(moe_loaded[j], 16)
            with sp.Fori(1, PAIRS) as pair:
                for j in range(MOER):
                    sp.wait_ge(moe_used[j], pair)
                    sp.dma_start(ring[:, MOE_SLOT[j], :], w_moe[pair, j]).then_inc(moe_loaded[j], 16)
            sp.wait_ge(routes, 1)
            end = sp.value_load(nsteps[0:1, 0:1], min_val=PAIRS, max_val=PAIRS * MAXQ)
            with sp.If(end > PAIRS):
                with sp.Fori(PAIRS, end, PAIRS) as first:
                    with sp.Fori(0, PAIRS) as pair:
                        for j in range(MOER):
                            sp.wait_ge(moe_used[j], first + pair)
                            sp.dma_start(ring[:, MOE_SLOT[j], :], w_moe[pair, j]).then_inc(moe_loaded[j], 16)
            for i in range(5):
                sp.wait_ge(moe_used[i], end)
                sp.dma_start(ring[:, MOE_SLOT[i], :], w_pleg[i] if i < 4 else w_ple).then_inc(ple_loaded, 16)
            sp.wait_ge(out_y, 16 * KD)
            for s, n in ((out_conf_p, 1), (out_ssm_p, 1), (out_h_p, 1), (out_conf_s, 1), (out_ssm_s, 1), (out_h_s, KD)):
                sp.wait_ge(s, 16 * n)

        @block.gpsimd
        def _(pool):
            g = nc.gpsimd
            g.memset(ident[:, :], 0.0)
            g.memset(mean_k[:, :], 1.0 / D)
            g.memset(mean_g[:, :], 1.0 / 256)
            g.memset(causal[:, :], 1.0)
            g.memset(eps[:, :], EPS)
            g.memset(glu[:, :, 0:KC - 1], 0.0)
            g.memset(xraw[:, :, 0:KS - 1], 0.0).then_inc(pool_self, 1)
            pool.wait_ge(pool_self, 1)
            g.affine_select(out=ident[:, :], in_=ident[:, :], compare_op=ALU.not_equal, fill=1.0, base=0,
                            pattern=[[-1, P]], channel_multiplier=1)
            g.affine_select(out=causal[:, :], in_=causal[:, :], compare_op=ALU.is_ge, fill=0.0, base=0,
                            pattern=[[1, P]], channel_multiplier=-1).then_inc(consts, 1)
            pool.dma_start(glu_s[:, :, 0:KC - 1, :], conf_s).then_inc(in_cs, 16)
            pool.dma_start(xraw_s[:, :, 0:KS - 1, :], ssm_s).then_inc(in_ss, 16)
            pool.dma_start(state, state_s).then_inc(in_st, 16)
            def new_states(i):
                pool.wait_ge(outer_ready, i + 1)
                g.tensor_tensor(state[:, i], state[:, i], outer[:, i % 2], ALU.add).then_inc(snew_ready, 1)
                pool.wait_ge(snew_ready, i + 1)
                pool.dma_start(h_s_out[:, i], state[:, i]).then_inc(out_h_s, 16)

            pool.wait_ge(in_cs, 16)
            for j in range(KD):
                pool.wait_ge(proj_evac, 2 * AT["g", j] + 2)
                g.tensor_tensor(glu[:, j, KC - 1:], asg[:, 0, j % 2, 0:NPR], asg[:, 1, j % 2, 0:NPR], ALU.mult)
                g.tensor_tensor(glu_s[:, j, KC - 1, :], asg[:, 0, j % 2, NPR:T], asg[:, 1, j % 2, NPR:T],
                                ALU.mult).then_inc(glu_ready, 1)
                if j == 3:
                    pool.wait_ge(proj_evac, 2 * NEARLY)
                    pool.dma_start(ssm_p_out, xraw[:, :, NPR:]).then_inc(out_ssm_p, 16)
                    pool.wait_ge(in_ss, 16)
                    pool.dma_start(ssm_s_out, xraw_s[:, :, 1:, :]).then_inc(out_ssm_s, 16)
                if j == 6:
                    new_states(0)
                    new_states(1)
            pool.wait_ge(glu_ready, KD)
            pool.dma_start(conf_p_out, glu[:, :, NPR:]).then_inc(out_conf_p, 16)
            pool.dma_start(conf_s_out, glu_s[:, :, 1:, :]).then_inc(out_conf_s, 16)
            for i in range(2, KD):
                new_states(i)
            pool.wait_ge(hp_done, NG)
            pool.dma_start(h_p_out, hst[:, :]).then_inc(out_h_p, 16)
            pool.wait_ge(m_out_ready, KD)
            pool.wait_ge(out_conf_p, 16)
            pool.dma_start(wr, w_router).then_inc(in_wr, 16)
            pool.dma_start(br, b_router).then_inc(in_wr, 16)
            g.memset(ones, 1.0)
            g.memset(before, 1.0)
            g.memset(r0[:, 0:528], 0.0)
            g.iota(iota_s, [[1, P]], base=0, channel_multiplier=0, allow_small_or_imprecise_dtypes=True)
            g.iota(iota4, [[1, 4]], base=0, channel_multiplier=0, allow_small_or_imprecise_dtypes=True)\
                .then_inc(pool_self, 1)
            pool.wait_ge(pool_self, 2)
            g.affine_select(out=before, in_=before, compare_op=ALU.is_gt, fill=0.0, base=0,
                            pattern=[[1, P]], channel_multiplier=-1).then_inc(consts, 1)
            for j in range(KD):
                pool.wait_ge(yo_ready, j + 1)
                pool.dma_start(yT[:, j], yo[:, j]).then_inc(out_y, 16)

        @block.scalar
        def _(act):
            a = nc.scalar
            n_self = [0]

            def link(ins):
                n_self[0] += 1
                ins.then_inc(act_self, 1)
                act.wait_ge(act_self, n_self[0])

            act.dma_start(h[:, :, :], xT).then_inc(in_x, 16)
            act.dma_start(prm[:, :], params).then_inc(in_prm, 16)
            act.dma_start(wdt[:, :, :], w_dt).then_inc(in_dt, 16)
            act.dma_start(hp[:, :], hparams).then_inc(in_h, 16)
            act.wait_ge(in_x, 16)
            a.activation(cat[:, 0:8, :], h[:, :, :], ACT.Square).then_inc(sq_ready, 1)

            def inv_root(i, bank, wait_sem, out_sem, n=1):
                act.wait_ge(wait_sem, i)
                act.wait_ge(consts, 1)
                link(a.activation(lnv[:, 0:n, :], ps[:, bank:bank + n, 0:T], ACT.Ln, bias=eps[:, 0:1]))
                a.activation(ps[:, bank:bank + n, 0:T], lnv[:, 0:n, :], ACT.Exp, scale=-0.5).then_inc(out_sem, 1)
                act.wait_ge(out_sem, i)

            inv_root(1, 4, stat_ready, rs_ready)
            act.wait_ge(dt_ready, 1)
            act.wait_ge(in_h, 16)
            a.activation(hs[:, 0, :], ps[0:NH, 7, 0:T], ACT.Identity, bias=hp[:, 0:1]).then_inc(dt_act, 1)
            act.wait_ge(dt_act, 1)
            a.activation(hs[:, 1, :], hs[:, 0, :], ACT.Abs).then_inc(dt_act, 1)
            act.wait_ge(dt_act, 2)
            a.activation(hs[:, 1, :], hs[:, 1, :], ACT.Exp, scale=-1.0).then_inc(dt_act, 1)
            a.activation(hp[:, 1:2], hp[:, 1:2], ACT.Exp).then_inc(dt_act, 1)
            def evacuate(s):
                kind, i = W_IN_ORDER[s]
                if kind == "g" and i >= 2:
                    act.wait_ge(glu_ready, i - 1)
                for q in range(2):
                    n = 2 * s + q
                    bank = n % 4 if s < NEARLY else n % 2
                    act.wait_ge(proj_ready, n + 1)
                    if kind == "g":
                        ins = a.activation(asg[:, q, i % 2, :], ps[:, bank, 0:T], ACT.Sigmoid if q else ACT.Copy)
                    elif kind == "x":
                        a.activation(xraw[:, 2 * i + q, KS - 1:], ps[:, bank, 0:NPR], ACT.Copy)
                        ins = a.activation(xraw_s[:, 2 * i + q, KS - 1, :], ps[:, bank, NPR:T], ACT.Copy)
                    else:
                        ins = a.activation(zs[:, 2 * i + q, :], ps[:, bank, 0:T], ACT.Silu)
                    ins.then_inc(proj_evac, 1)

            act.wait_ge(pool_self, 1)
            for s in range(NEARLY):
                evacuate(s)
                if s == 5:
                    act.wait_ge(dt_dve, 1)
                    for c in range(2):
                        a.activation(hs[:, 4, c * Q:(c + 1) * Q], hs[:, 3, c * Q:(c + 1) * Q], ACT.Exp, scale=-1.0,
                                     bias=hs[:, 3, (c + 1) * Q - 1:(c + 1) * Q])
                    a.activation(hs[:, 4, NPR:T], hs[:, 5, NPR:T], ACT.Exp).then_inc(dt_act, 1)

            def exp_of(i):
                act.wait_ge(dif_ready, i + 1)
                a.activation(mexp[:, i % 2, :, :], mexp[:, i % 2, :, :], ACT.Exp).then_inc(exp_ready, 1)

            def exp_carry(i):
                if i > NG:
                    act.wait_ge(y_psum, i)
                a.activation(ea[:, :, :], ps[:, BC[i % 2], :].rearrange("p (r n) -> p r n", r=4), ACT.Exp)\
                    .then_inc(ea_ready, 1)

            def decode(i):
                if i == 0:
                    act.wait_ge(in_st, 16)
                    act.wait_ge(dtx_ready, 1)
                for b in range(NSM):
                    a.activation(state[:, i, b, :], state[:, i, b, :], ACT.Copy, scale=chd[:, i, 8 + b:9 + b])
                act.wait_ge(bbc_psum, i // 2 + 1)
                if i >= 2:
                    act.wait_ge(snew_ready, i - 1)
                for b in range(NSM):
                    ins = a.activation(outer[:, i % 2, b, :], ps[:, 2 + b // 4, (b % 4) * P:(b % 4 + 1) * P], ACT.Copy,
                                       scale=dtx[:, i, b:b + 1])
                ins.then_inc(outer_ready, 1)

            def keep_c(gr):
                act.wait_ge(cbc_psum, gr + 1)
                if gr >= 2:
                    act.wait_ge(y_s_ready, 2 * gr - 2)
                a.activation(cbc[:, gr % 2].rearrange("p (a b) n -> p a (b n)", a=2), ps[:, 2:4, :], ACT.Copy)\
                    .then_inc(cbc_ready, 1)

            evacuate(NEARLY)
            evacuate(NEARLY + 1)
            for m in range(0, NX, 2):
                act.wait_ge(xconv_done, m // 2 + 1)
                a.activation(xbc[:, m:m + 2, 0:NPR], xbc[:, m:m + 2, 0:NPR], ACT.Silu).then_inc(xbc_ready, 1)
            act.wait_ge(xconv_done, NX // 2 + 1)
            a.activation(xbc[:, :, NPR:T], xbc[:, :, NPR:T], ACT.Silu).then_inc(xbc_ready, 1)
            for c in range(2):
                act.wait_ge(btok_psum, c + 1)
                a.activation(btok[:, c, :, :], ps[:, BC[c], :].rearrange("p (g n) -> p g n", g=NG), ACT.Copy)\
                    .then_inc(btok_ready, 1)
            exp_of(0)
            for i in range(2 * NG):
                if i + 1 < 2 * NG:
                    exp_of(i + 1)
                    if i + 1 >= NG:
                        exp_carry(i + 1)
                if i % 2 == 0:
                    decode(i)
                    decode(i + 1)
                else:
                    keep_c(i // 2)
                if i in SLOT_AFTER:
                    evacuate(SLOT_AFTER[i])
            act.wait_ge(ln_xc, 1)
            act.wait_ge(out_conf_p, 16)
            a.activation(glu[:, :, 0:T], cat[:, 0:8, :], ACT.Square).then_inc(ln_sq, 1)
            inv_root(1, 2, ln_var, ln_rs)
            act.wait_ge(ln_n, 1)
            for j in range(KD):
                a.activation(cat[:, j, :], cat[:, j, :], ACT.Silu, scale=par("ln_g", j), bias=par("ln_b", j))\
                    .then_inc(a_out_ready, 1)
            act.wait_ge(ycat_ready, 1)
            a.activation(u[:, :, :], cat[:, 8:16, :], ACT.Square).then_inc(gsq_ready, 1)
            inv_root(1, 0, gstat, grs, n=NG)
            act.wait_ge(o_added, KD)
            a.activation(cat[:, 0:8, :], h[:, :, :], ACT.Square).then_inc(sq_ready, 1)
            inv_root(2, 4, stat_ready, rs_ready)
            act.dma_start(pt, pT).then_inc(in_p, 16)
            act.wait_ge(r_dve, 1)
            a.activation(gexp, gd, ACT.Exp).then_inc(r_act, 1)
            act.wait_ge(r_dve, 2)
            a.activation(e2, t1, ACT.Exp).then_inc(r_act, 1)
            for t in range(2):
                act.wait_ge(utok_psum, t + 1)
                a.activation(utok[:, t, :].rearrange("p (b n) -> p b n", b=2), ps[:, 2 * t:2 * t + 2, :], ACT.Copy)\
                    .then_inc(utok_ready, 1)
            act.wait_ge(xg_psum, 1)
            a.activation(xg.rearrange("p (b c) n -> p b (c n)", b=2), ps[:, 5:7, :], ACT.Copy).then_inc(xg_ready, 1)
            act.wait_ge(routes, 1)
            end = act.value_load(nsteps[0:1, 1:2], min_val=PAIRS + 1, max_val=PAIRS * MAXQ + 1)
            steps = act.value_load(nsteps[0:1, 0:1], min_val=PAIRS, max_val=PAIRS * MAXQ)
            with act.Fori(1, end) as step:
                act.wait_ge(gate_done, step)
                a.activation(silu_e, ps[:, 0, :], ACT.Silu).then_inc(silu_ready, 1)
                act.wait_ge(xg_psum, step + 1)
                a.activation(xg.rearrange("p (b c) n -> p b (c n)", b=2), ps[:, 5:7, :], ACT.Copy).then_inc(xg_ready, 1)
                act.wait_ge(hidt_psum, step)
                a.activation(hidt, ps[:, 2, :].rearrange("p (k n) -> p k n", k=4), ACT.Copy).then_inc(hidt_ready, 1)
                act.wait_ge(down_done, step)
                a.activation(ysb.rearrange("p (b c) n -> p b (c n)", b=2), ps[:, 3:5, :], ACT.Copy)\
                    .then_inc(ytok_ready, 1)
            act.wait_ge(sc_added[0], 4 * steps + 1)
            act.wait_ge(sc_added[1], 4 * steps + 1)
            a.activation(cat[:, 0:8, :], h[:, :, :], ACT.Square).then_inc(sq_ready, 1)
            inv_root(3, 4, stat_ready, rs_ready)
            for j in range(KD):
                act.wait_ge(gate_psum, j + 1)
                if j >= 2:
                    act.wait_ge(h_ple, j - 1)
                a.activation(sg[:, j % 2, :], ps[:, j % 2, 0:T], ACT.Sigmoid).then_inc(gate_sig, 1)
            act.wait_ge(h_ple, KD)
            a.activation(cat[:, 0:8, :], h[:, :, :], ACT.Square).then_inc(sq_ready, 1)
            inv_root(4, 4, stat_ready, rs_ready)

        @block.tensor
        def _(pe):
            mm = nc.tensor.matmul
            tr = nc.tensor.transpose

            def mean_of(x, bank, w, n0=0, n=KD):
                for k in range(n):
                    ins = mm(ps[:, bank, 0:T], w[:, :], x[:, n0 + k, 0:T], start=(k == 0), stop=(k == n - 1))
                return ins

            pe.wait_ge(consts, 1)
            pe.wait_ge(sq_ready, 1)
            mean_of(cat, 4, mean_k).then_inc(stat_ready, 1)
            pe.wait_ge(in_dt, 16)
            for k in range(KD):
                pe.wait_ge(u_ready, k + 1)
                ins = mm(ps[0:NH, 7, 0:T], wdt[:, k, :], u[:, k, :], start=(k == 0), stop=(k == KD - 1))
            ins.then_inc(dt_ready, 1)
            def project(s):
                pe.wait_ge(mix_loaded[s % MIXR], 16 * (s // MIXR + 1))
                wv = ring[:, s % MIXR, :].rearrange("p (k n) -> p k n", k=KD)
                for q in range(2):
                    n = 2 * s + q
                    if n >= 4:
                        pe.wait_ge(proj_evac, n - 3 if s <= NEARLY else n - 1)
                    for k in range(KD):
                        ins = mm(ps[:, n % (4 if s < NEARLY else 2), 0:T], wv[:, k, q * P:(q + 1) * P], u[:, k, :],
                                 start=(k == 0), stop=(k == KD - 1))
                    ins.then_inc(proj_ready, 1)

            def spread(i):
                c, gr = divmod(i, NG)
                if i < 2:
                    pe.wait_ge(btok_ready, i + 1)
                else:
                    pe.wait_ge(dif_ready, i - 1)
                    if i - 2 >= NG:
                        pe.wait_ge(ea_ready, i - 2 - NG + 1)
                for r in range(4):
                    hd = 4 * gr + r
                    ins = mm(ps[:, BC[i % 2], r * P:(r + 1) * P], ident[0:NH, hd:hd + 1].to_broadcast([NH, P]),
                             hs[:, 3, c * Q:(c + 1) * Q], start=True, stop=True)
                ins.then_inc(bc_psum, 1)

            def item(i):
                c, gr = divmod(i, NG)
                bank = 5 + i % 2
                pe.wait_ge(m_ready, i + 1)
                if c == 1:
                    pe.wait_ge(ce_ready, gr + 1)
                if i >= 2:
                    pe.wait_ge(y_ready, i - 1)
                else:
                    pe.wait_ge(cb_ready, i + 1)
                for r in range(4):
                    hd = 4 * gr + r
                    q = (r % 2) * HD
                    o = ps[q:q + HD, bank, (r // 2) * P:(r // 2 + 1) * P]
                    mm(o, xdt[:, c, hd * HD:(hd + 1) * HD], mexp[:, i % 2, r, :], start=True, stop=(c == 0))
                    if c == 1:
                        mm(o, hst[:, hd * HD:(hd + 1) * HD], ea[:, r, :], start=False, stop=True)
                mm(ps[:, bank, 256:512], btok[:, c, gr, :], xdec[:, c, gr * 256:(gr + 1) * 256],
                   start=True, stop=True).then_inc(y_psum, 1)

            def spread_rows(m, gr, out_sem):
                if m == 12:
                    pe.wait_ge(outer_ready, 2 * gr + 2)
                elif gr:
                    pe.wait_ge(cbc_ready, gr)
                else:
                    pe.wait_ge(xtok_ready, 4)
                    pe.wait_ge(xbc_ready, NX // 2 + 1)
                for b in range(NSM):
                    ins = mm(ps[:, 2 + b // 4, (b % 4) * P:(b % 4 + 1) * P],
                             xbc[:, m + gr, NPR + b:NPR + b + 1].to_broadcast([P, P]), ident[:, :], start=True, stop=True)
                ins.then_inc(out_sem, 1)

            for s in range(NEARLY + 2):
                project(s)
            pe.wait_ge(hrow_ready, 1)
            for v, row in enumerate((2, 1, 0)):
                for c in range(2):
                    ins = tr(ps[:, 7, (2 * v + c) * NH:(2 * v + c + 1) * NH], hs[:, row, c * Q:(c + 1) * Q],
                             ident[0:NH, 0:NH])
            for hd in range(NH):
                j, q = hd // 2, HD * (hd % 2)
                ins = mm(ps[q:q + HD, 7, P + 16 * j:P + 16 * j + 16], ident[0:NH, hd:hd + 1].to_broadcast([NH, HD]),
                         hs[:, 2:6:2, NPR:T], start=True, stop=True)
            ins.then_inc(htok_psum, 1)
            pe.wait_ge(proj_evac, 2 * NEARLY)
            for c in range(2):
                for hf in range(2):
                    for j in range(4):
                        if c == 0:
                            pe.wait_ge(xbc_ready, (4 * hf + j) // 2 + 1)
                        ins = tr(ps[:, XT[2 * c + hf], j * P:(j + 1) * P], xbc[:, 4 * hf + j, c * Q:(c + 1) * Q],
                                 ident[:, :])
                    ins.then_inc(xtok_psum, 1)
            pe.wait_ge(xbc_ready, NX // 2)
            for c in range(2):
                if c == 1:
                    pe.wait_ge(htok_ready, 1)
                for gr in range(NG):
                    ins = tr(ps[:, BC[c], gr * P:(gr + 1) * P], xbc[:, 8 + gr, c * Q:(c + 1) * Q], ident[:, :])
                ins.then_inc(btok_psum, 1)
            for c in range(2):
                pe.wait_ge(xtok_ready, 3 + c)
                for gr in range(NG):
                    ins = mm(ps[:, 5 + c, gr * P:(gr + 1) * P], xbc[:, 8 + gr, c * Q:(c + 1) * Q],
                             xbc[:, 12 + gr, c * Q:(c + 1) * Q], start=True, stop=True)
                ins.then_inc(cb_psum, 1)
            spread(0)
            spread(1)
            for i in range(2 * NG):
                item(i)
                if i + 2 < 2 * NG:
                    spread(i + 2)
                if i % 2 == 0:
                    spread_rows(8, i // 2, bbc_psum)
                else:
                    spread_rows(12, i // 2, cbc_psum)
                if i in SLOT_AFTER:
                    project(SLOT_AFTER[i])
            pe.wait_ge(conv_done, KD)
            pe.wait_ge(conv_s_done, KD)
            pe.wait_ge(cbc_ready, NG)
            mean_of(cat, 2, mean_k).then_inc(ln_mean, 1)
            pe.wait_ge(ln_sq, 1)
            mean_of(glu, 2, mean_k).then_inc(ln_var, 1)
            pe.wait_ge(gsq_ready, 1)
            pe.wait_ge(ln_n, 1)
            pe.wait_ge(proj_evac, 2 * NWIN)
            for gr in range(NG):
                ins = mean_of(u, gr, mean_g, n0=2 * gr, n=2)
            ins.then_inc(gstat, 1)
            for n in range(KD):
                s = NWIN + n
                pe.wait_ge(mix_loaded[s % MIXR], 16 * (s // MIXR + 1))
                if n == 0:
                    pe.wait_ge(a_out_ready, KD)
                    pe.wait_ge(m_out_ready, KD)
                if n >= 4:
                    pe.wait_ge(o_added, n - 3)
                wv = ring[:, s % MIXR, :].rearrange("p (k n) -> p k n", k=16)
                for k in range(16):
                    ins = mm(ps[:, 4 + n % 4, 0:T], wv[:, k, :], cat[:, k, :], start=(k == 0), stop=(k == 15))
                ins.then_inc(o_psum, 1)
            pe.wait_ge(sq_ready, 2)
            mean_of(cat, 4, mean_k).then_inc(stat_ready, 1)
            pe.wait_ge(in_wr, 32)
            pe.wait_ge(u_ready, 2 * KD)
            for t, (t0, tn) in enumerate(TOK):
                for k in range(KD):
                    ins = mm(ps[0:tn, 7, 20 * t:20 * t + 20], u[:, k, t0:t0 + tn], wr[:, k, :],
                             start=(k == 0), stop=(k == KD - 1))
            ins.then_inc(log_psum, 1)
            for t, (t0, tn) in enumerate(TOK):
                if t == 2:
                    pe.wait_ge(u_ready, 2 * KD)
                for j in range(KD):
                    ins = tr(ps[0:tn, 2 * t + j // 4, (j % 4) * P:(j % 4 + 1) * P], u[:, j, t0:t0 + tn], ident[:, :])
                ins.then_inc(utok_psum, 1)
            pe.wait_ge(assigned, 1)
            pe.wait_ge(consts, 2)
            for t, (t0, tn) in enumerate(TOK):
                for v in range(t + 1):
                    vn = TOK[v][1]
                    ins = mm(ps[0:tn, 6, 16 * t:16 * t + 16], (before if v == t else ones)[0:vn, 0:tn],
                             a12[0:vn, v, :], start=(v == 0), stop=(v == t))
            for v, (_, vn) in enumerate(TOK):
                ins = mm(ps[:, 6, 48:64], ones[0:vn, :], a12[0:vn, v, :], start=(v == 0), stop=(v == 2))
            ins.then_inc(pos_psum, 1)

            def gather():
                for c in range(KD):
                    for t, (_, tn) in enumerate(TOK):
                        ins = mm(ps[:, 5 + c // 4, (c % 4) * P:(c % 4 + 1) * P], utok[0:tn, t, c * P:(c + 1) * P],
                                 sel[0:tn, t, :], start=(t == 0), stop=(t == 2))
                ins.then_inc(xg_psum, 1)

            pe.wait_ge(utok_ready, 3)
            pe.wait_ge(sel_ready, 1)
            gather()
            pe.wait_ge(routes, 1)
            end = pe.value_load(nsteps[0:1, 1:2], min_val=PAIRS + 1, max_val=PAIRS * MAXQ + 1)
            steps = pe.value_load(nsteps[0:1, 0:1], min_val=PAIRS, max_val=PAIRS * MAXQ)
            with pe.Fori(1, end) as step:
                pe.wait_ge(xg_ready, step)
                pe.wait_ge(selt_ready, step)
                for gu in range(2):
                    for hf in range(2):
                        for k in range(4):
                            for e in range(2):
                                j = 4 * gu + 2 * hf + e
                                if k == 0:
                                    pe.wait_ge(moe_loaded[j], 16 * step)
                                wv = ring[:, MOE_SLOT[j], :].rearrange("p (k n) -> p k n", k=4)
                                ins = mm(ps[e * CAP:(e + 1) * CAP, gu, :], xg[:, 4 * hf + k, e * CAP:(e + 1) * CAP],
                                         wv[:, k, :], start=(hf == 0 and k == 0), stop=(hf == 1 and k == 3))
                                if k == 3:
                                    ins.then_inc(moe_used[j], 1)
                pe.wait_ge(selw_ready, step)
                pe.wait_ge(silu_ready, step)
                for t, (t0, tn) in enumerate(TOK):
                    ins = tr(ps[:, 0, t0:t0 + tn], selw[0:tn, t, :], ident[0:tn, 0:tn])
                ins.then_inc(selt_psum, 1)
                pe.wait_ge(sel_ready, step + 1)
                gather()
                pe.wait_ge(hid_ready, step)
                pe.wait_ge(sc_added[1], 4 * step - 3)
                for k in range(4):
                    ins = tr(ps[:, 2, k * P:(k + 1) * P], hid[:, k * P:(k + 1) * P], ident[:, :])
                ins.then_inc(hidt_psum, 1)
                pe.wait_ge(hidt_ready, step)
                for hf in range(2):
                    for k in range(2):
                        for e in range(2):
                            j = 8 + 2 * hf + e
                            if k == 0:
                                pe.wait_ge(moe_loaded[j], 16 * step)
                            wv = ring[:, MOE_SLOT[j], :].rearrange("p (k n) -> p k n", k=2)
                            for o in range(2):
                                ins = mm(ps[e * CAP:(e + 1) * CAP, 3 + o, :], hidt[:, 2 * hf + k, e * CAP:(e + 1) * CAP],
                                         wv[:, k, o * 512:(o + 1) * 512], start=(hf == 0 and k == 0),
                                         stop=(hf == 1 and k == 1))
                            if k == 1:
                                ins.then_inc(moe_used[j], 1)
                pe.wait_ge(ytok_ready, step)
                pe.wait_ge(selt_ready, step + 1)
                for c in range(KD):
                    pe.wait_ge(sc_added[c % 2], 4 * step - 3 + c // 2)
                    mm(ps[:, SC[c % 2], 0:T], ysb[:, c, :], selt, start=True, stop=True).then_inc(sc_psum[c % 2], 1)
            pe.wait_ge(sq_ready, 3)
            pe.wait_ge(ytok_ready, steps)
            mean_of(cat, 4, mean_k).then_inc(stat_ready, 1)
            pe.wait_ge(ple_loaded, 16 * 5)
            pe.wait_ge(in_p, 16)
            pe.wait_ge(sc_added[1], 4 * steps + 1)
            wp = ring[:, MOE_SLOT[4], :].rearrange("p (k n) -> p k n", k=2)
            for j in range(KD):
                if j >= 2:
                    pe.wait_ge(gate_mul, j - 1)
                for k in range(2):
                    mm(ps[:, 2 + j % 2, 0:T], wp[:, k, j * P:(j + 1) * P], pt[:, k, :], start=(k == 0), stop=(k == 1))
                if j == 0:
                    pe.wait_ge(u_ready, 3 * KD)
                wv = ring[:, MOE_SLOT[j // 2], :].rearrange("p (k n) -> p k n", k=KD)
                for k in range(KD):
                    ins = mm(ps[:, j % 2, 0:T], wv[:, k, (j % 2) * P:(j % 2 + 1) * P], u[:, k, :],
                             start=(k == 0), stop=(k == KD - 1))
                ins.then_inc(gate_psum, 1)
            pe.wait_ge(sq_ready, 4)
            mean_of(cat, 4, mean_k).then_inc(stat_ready, 1)

        @block.vector
        def _(dve):
            v = nc.vector
            n_self = [0]

            def link(ins):
                n_self[0] += 1
                ins.then_inc(dve_self, 1)
                dve.wait_ge(dve_self, n_self[0])

            def mark(ins):
                n_self[0] += 1
                ins.then_inc(dve_self, 1)
                return n_self[0]

            def normed(out, gain, i, out_sem, wait=True):
                dve.wait_ge(rs_ready, i)
                for j in range(KD):
                    v.scalar_tensor_tensor(out=out[:, j, :], in0=h[:, j, :], scalar=par(gain, j), in1=ps[:, 4, 0:T],
                                           op0=ALU.mult, op1=ALU.mult).then_inc(out_sem, 1)

            dve.wait_ge(in_prm, 16)
            dve.wait_ge(in_x, 16)
            normed(u, "g_mix", 1, u_ready)
            X, E, DT, ACS, DEC, A = range(6)
            dve.wait_ge(dt_act, 4)
            link(v.tensor_scalar(hs[:, A, :], hs[:, E, :], 2.0, None, ALU.add))
            link(v.reciprocal(hs[:, A, :], hs[:, A, :]))
            link(v.tensor_tensor(hs[:, E, :], hs[:, E, :], hs[:, A, :], ALU.mult))
            link(v.tensor_tensor(hs[:, A, :], hs[:, E, :], hs[:, E, :], ALU.mult))
            link(v.tensor_scalar(hs[:, DT, :], hs[:, A, :], 1.0 / 17, None, ALU.mult))
            for k in range(15, 1, -2):
                link(v.scalar_tensor_tensor(out=hs[:, DT, :], in0=hs[:, DT, :], scalar=1.0 / k, in1=hs[:, A, :],
                                            op0=ALU.add, op1=ALU.mult))
            link(v.scalar_tensor_tensor(out=hs[:, DT, :], in0=hs[:, DT, :], scalar=1.0, in1=hs[:, E, :],
                                        op0=ALU.add, op1=ALU.mult))
            link(v.tensor_scalar(hs[:, X, :], hs[:, X, :], 0.0, None, ALU.max))
            link(v.scalar_tensor_tensor(out=hs[:, DT, :], in0=hs[:, DT, :], scalar=2.0, in1=hs[:, X, :],
                                        op0=ALU.mult, op1=ALU.add))
            link(v.tensor_scalar(hs[:, A, :], hs[:, DT, :], hp[:, 1:2], -1.0, ALU.mult, ALU.mult))
            dve.wait_ge(consts, 1)
            link(v.tensor_scalar(hs[:, X, 0:Q], hs[:, A, 0:Q], 0.0, 1.0, ALU.mult, ALU.add))
            for c in range(2):
                ins = v.tensor_tensor_scan(hs[:, ACS, c * Q:(c + 1) * Q], hs[:, X, 0:Q], hs[:, A, c * Q:(c + 1) * Q],
                                           0.0, ALU.mult, ALU.add)
            ins.then_inc(dt_dve, 1)
            dve.wait_ge(dt_dve, 1)
            v.tensor_scalar(hs[:, X, 0:NPR], hs[:, ACS, 0:NPR], -1.0, None, ALU.mult)

            def decode_conv_x():
                dve.wait_ge(in_ss, 16)
                pr = prod[:, :].rearrange("p (m k b) -> p m k b", m=8, k=KS)
                xw = par("xconv_w", 0, NX * KS).rearrange("p (m k) -> p m k", m=NX)
                for m in (0, 8):
                    link(v.tensor_tensor(pr, xraw_s[:, m:m + 8], xw[:, m:m + 8].unsqueeze(3).to_broadcast([P, 8, KS, NSM]),
                                         ALU.mult))
                    link(v.tensor_reduce(xbc[:, m:m + 8, NPR:T], pr.rearrange("p m k b -> p m b k"), AX.X, ALU.add))
                v.tensor_tensor(xbc[:, :, NPR:T], xbc[:, :, NPR:T],
                                par("xconv_b", 0, NX).unsqueeze(2).to_broadcast([P, NX, NSM]), ALU.add)\
                    .then_inc(xconv_done, 1)

            cw = par("conv_w", 0, KD * KC)

            def decode_conv(j):
                dve.wait_ge(glu_ready, j + 1)
                pr = prod[:, 0:KC * NSM].rearrange("p (k b) -> p k b", k=KC)
                link(v.tensor_tensor(pr, glu_s[:, j], cw[:, j * KC:(j + 1) * KC].unsqueeze(2).to_broadcast([P, KC, NSM]),
                                     ALU.mult))
                link(v.tensor_reduce(cat[:, j, NPR:T], pr.rearrange("p k b -> p b k"), AX.X, ALU.add))
                v.tensor_scalar(cat[:, j, NPR:T], cat[:, j, NPR:T], par("conv_b", j), None, ALU.add)\
                    .then_inc(conv_s_done, 1)

            def conv_x(m):
                dve.wait_ge(proj_evac, 2 * AT["x", m // 2] + 2)
                if m:
                    dve.wait_ge(xconv_done, m // 2)
                at = [0, 0]
                for k in range(KS):
                    for q in range(2):
                        src, w = xraw[:, m + q, k:k + NPR], par("xconv_w", (m + q) * KS + k)
                        acc = ps[:, 5 + q, 0:NPR]
                        if k == 0:
                            at[q] = mark(v.tensor_scalar(acc, src, w, par("xconv_b", m + q), ALU.mult, ALU.add))
                            continue
                        dve.wait_ge(dve_self, at[q])
                        ins = v.scalar_tensor_tensor(out=xbc[:, m + q, 0:NPR] if k == KS - 1 else acc, in0=src,
                                                     scalar=w, in1=acc, op0=ALU.mult, op1=ALU.add)
                        if k < KS - 1:
                            at[q] = mark(ins)
                ins.then_inc(xconv_done, 1)

            at_tap = [0, 0]

            def conv(j, k0, k1):
                if k0 == 0:
                    dve.wait_ge(glu_ready, j + 1)
                    if j:
                        dve.wait_ge(conv_done, j)
                    if j > 4:
                        dve.wait_ge(conv_s_done, j)
                    if j > 5:
                        dve.wait_ge(y_s_ready, 2 * (j - 5))
                for k in range(k0, k1):
                    src, w, q = glu[:, j, k:k + NPR], par("conv_w", j * KC + k), k % 2
                    acc = prod[:, :] if q else cat[:, j, 0:NPR]
                    if k < 2:
                        ins = v.tensor_scalar(acc, src, w, None if q else par("conv_b", j), ALU.mult,
                                              *(() if q else (ALU.add,)))
                    else:
                        dve.wait_ge(dve_self, at_tap[q])
                        ins = v.scalar_tensor_tensor(out=acc, in0=src, scalar=w, in1=acc, op0=ALU.mult, op1=ALU.add)
                    at_tap[q] = mark(ins)
                if k1 == KC:
                    dve.wait_ge(dve_self, at_tap[0])
                    v.tensor_tensor(cat[:, j, 0:NPR], cat[:, j, 0:NPR], prod[:, :], ALU.add).then_inc(conv_done, 1)

            for q in range(4):
                conv(q, 0, KC)
                conv_x(4 * q)
                conv_x(4 * q + 2)
            dve.wait_ge(conv_done, 4)
            decode_conv_x()
            dve.wait_ge(xconv_done, 9)
            for j in range(4):
                decode_conv(j)
                dve.wait_ge(conv_s_done, j + 1)
            dve.wait_ge(dt_act, 5)
            v.tensor_tensor(hs[:, E, 0:NPR], hs[:, DT, 0:NPR], hs[:, DEC, 0:NPR], ALU.mult).then_inc(hrow_ready, 1)
            dve.wait_ge(htok_psum, 1)
            v.tensor_copy(chd[:, :, :], ps[:, 7, P:2 * P].rearrange("p (j n) -> p j n", j=KD))
            v.tensor_copy(htok[:, :, :], ps[:, 7, 0:6 * NH].rearrange("p (v n) -> p v n", v=6)).then_inc(htok_ready, 1)
            dve.wait_ge(htok_ready, 1)
            dve.wait_ge(out_ssm_p, 16)
            for i in range(4):
                c, hf = divmod(i, 2)
                dve.wait_ge(xtok_psum, i + 1)
                src = ps[:, XT[i], :].rearrange("p (h d) -> p h d", h=8)
                for dst, row in ((xdt, c), (xdec, 2 + c)):
                    ins = v.tensor_tensor(dst[:, c, hf * 512:(hf + 1) * 512].rearrange("p (h d) -> p h d", h=8), src,
                                          htok[:, row, hf * 8:hf * 8 + 8].unsqueeze(2).to_broadcast([P, 8, HD]), ALU.mult)
                ins.then_inc(xtok_ready, 1)
            for c in range(2):
                dve.wait_ge(cb_psum, c + 1)
                v.tensor_tensor(cbm[:, c, :, :], ps[:, 5 + c, :].rearrange("p (g n) -> p g n", g=NG),
                                causal.unsqueeze(1).to_broadcast([P, NG, P]), ALU.mult).then_inc(cb_ready, 1)
            dve.wait_ge(cb_ready, 2)

            def spread_done(i):
                c, gr = divmod(i, NG)
                dve.wait_ge(exp_ready, i + 1)
                v.tensor_tensor(mexp[:, i % 2, :, :], mexp[:, i % 2, :, :],
                                cbm[:, c, gr, :].unsqueeze(1).to_broadcast([P, 4, P]), ALU.mult).then_inc(m_ready, 1)
                if c == 1:
                    dve.wait_ge(ea_ready, gr + 1)
                    link(v.tensor_copy(cdec[:, :], ea[:, :, P - 1]))
                    v.tensor_tensor(ea[:, :, :], ea[:, :, :],
                                    xbc[:, 12 + gr, Q:2 * Q].unsqueeze(1).to_broadcast([P, 4, P]), ALU.mult)\
                        .then_inc(ce_ready, 1)

            def take(i):
                c, gr = divmod(i, NG)
                bank = 5 + i % 2
                dve.wait_ge(y_psum, i + 1)
                cols = slice(gr * 256, (gr + 1) * 256)
                if c == 0:
                    v.tensor_copy(hst[:, cols], ps[:, bank, 256:512]).then_inc(st_ready, 1)
                else:
                    hv = hst[:, cols].rearrange("p (r d) -> p r d", r=4)
                    link(v.tensor_tensor(hv, hv, cdec[:, :].unsqueeze(2).to_broadcast([P, 4, HD]), ALU.mult))
                    v.tensor_tensor(hst[:, cols], hst[:, cols], ps[:, bank, 256:512], ALU.add).then_inc(hp_done, 1)
                for jj in range(2):
                    j = 2 * gr + jj
                    ins = v.scalar_tensor_tensor(out=cat[:, 8 + j, c * Q:(c + 1) * Q], in0=xbc[:, j, c * Q:(c + 1) * Q],
                                                 scalar=par("d_skip", j), in1=ps[:, bank, jj * P:(jj + 1) * P],
                                                 op0=ALU.mult, op1=ALU.add)
                ins.then_inc(y_ready, 1)

            def difference(i):
                c, gr = divmod(i, NG)
                dve.wait_ge(bc_psum, i + 1)
                if i >= 2:
                    dve.wait_ge(y_psum, i - 1)
                for r in range(4):
                    hd = 4 * gr + r
                    ins = v.tensor_scalar(mexp[:, i % 2, r, :], ps[:, BC[i % 2], r * P:(r + 1) * P],
                                          htok[:, 4 + c, hd:hd + 1], 0.0, ALU.add, ALU.min)
                ins.then_inc(dif_ready, 1)

            def decode(i):
                dve.wait_ge(snew_ready, i + 1)
                dve.wait_ge(cbc_ready, i // 2 + 1)
                for b in range(NSM):
                    if b:
                        dve.wait_ge(ttr_done, NSM * i + b)
                    v.tensor_tensor_reduce(out=prod[:, 0:P], in0=state[:, i, b, :],
                                           in1=cbc[:, i // 2 % 2, b, :], scale=1.0, scalar=0.0,
                                           op0=ALU.mult, op1=ALU.add, accum_out=cat[:, 8 + i, NPR + b:NPR + b + 1])\
                        .then_inc(ttr_done, 1)
                dve.wait_ge(ttr_done, NSM * (i + 1))
                v.scalar_tensor_tensor(out=cat[:, 8 + i, NPR:T], in0=xbc[:, i, NPR:T], scalar=par("d_skip", i),
                                       in1=cat[:, 8 + i, NPR:T], op0=ALU.mult, op1=ALU.add).then_inc(y_s_ready, 1)

            dve.wait_ge(xbc_ready, NX // 2 + 1)
            v.tensor_tensor(dtx[:, :, :], xbc[:, 0:KD, NPR:T], chd[:, :, 0:8], ALU.mult).then_inc(dtx_ready, 1)
            difference(0)
            for i in range(2 * NG):
                j = 4 + i // 2
                cuts = [0, 8, 16] if i % 2 == 0 else [16, 24, KC]
                if i == NG:
                    dve.wait_ge(st_ready, NG)
                if i + 1 < 2 * NG:
                    difference(i + 1)
                conv(j, cuts[0], cuts[1])
                spread_done(i)
                conv(j, cuts[1], cuts[2])
                take(i)
                if i % 2:
                    dve.wait_ge(conv_done, j + 1)
                    decode_conv(j)
                    if i >= 3:
                        dve.wait_ge(conv_s_done, j + 1)
                        decode(i - 3)
                        decode(i - 2)
            decode(6)
            decode(7)
            dve.wait_ge(y_s_ready, KD)
            dve.wait_ge(ln_mean, 1)
            v.tensor_tensor(cat[:, 0:8, :], cat[:, 0:8, :],
                            ps[:, 2, 0:T].unsqueeze(1).to_broadcast([P, KD, T]), ALU.subtract).then_inc(ln_xc, 1)
            dve.wait_ge(proj_evac, 2 * NWIN)
            v.tensor_tensor(cat[:, 8:16, :], cat[:, 8:16, :], zs, ALU.mult).then_inc(ycat_ready, 1)
            dve.wait_ge(ln_rs, 1)
            v.tensor_tensor(cat[:, 0:8, :], cat[:, 0:8, :],
                            ps[:, 2, 0:T].unsqueeze(1).to_broadcast([P, KD, T]), ALU.mult).then_inc(ln_n, 1)
            dve.wait_ge(ycat_ready, 1)
            dve.wait_ge(grs, 1)
            for j in range(KD):
                v.scalar_tensor_tensor(out=cat[:, 8 + j, :], in0=cat[:, 8 + j, :], scalar=par("ssm_g", j),
                                       in1=ps[:, j // 2, 0:T], op0=ALU.mult, op1=ALU.mult).then_inc(m_out_ready, 1)
            for n in range(KD):
                dve.wait_ge(o_psum, n + 1)
                v.tensor_tensor(h[:, n, :], h[:, n, :], ps[:, 4 + n % 4, 0:T], ALU.add).then_inc(o_added, 1)
            dve.wait_ge(o_added, KD)
            normed(u, "g_ffn", 2, u_ready)

            dve.wait_ge(consts, 2)
            dve.wait_ge(log_psum, 1)
            v.tensor_tensor(logit[:, 0:2, :], ps[:, 7, 0:40].rearrange("p (t n) -> p t n", t=2),
                            br.unsqueeze(1).to_broadcast([P, 2, 20]), ALU.add)
            link(v.tensor_tensor(logit[0:NSM, 2, :], ps[0:NSM, 7, 40:60], br[0:NSM, :], ALU.add))
            b4 = lambda x: x.to_broadcast([P, 3, 4])
            i4 = iota4.unsqueeze(1).to_broadcast([P, 3, 4])
            link(v.tensor_reduce(gmax, logit[:, :, 0:4], AX.X, ALU.max))
            v.tensor_tensor(gd, logit[:, :, 0:4], b4(gmax), ALU.subtract).then_inc(r_dve, 1)
            dve.wait_ge(r_dve, 1)

            def first_of(d, c, low, onehot):
                link(v.tensor_scalar(c, d, 0.0, -8.0, ALU.is_ge, ALU.mult))
                link(v.tensor_tensor(c, c, i4, ALU.add))
                link(v.tensor_reduce(low, c, AX.X, ALU.min))
                link(v.tensor_tensor(onehot, c, b4(low), ALU.is_equal))

            first_of(gd, gc, gmin, gsel)
            lev = logit[:, :, 4:20].rearrange("p t (g e) -> p t g e", g=4)
            pv = prod16.rearrange("p t (g e) -> p t g e", g=4)
            link(v.tensor_tensor(pv, lev, gsel.unsqueeze(3).to_broadcast([P, 3, 4, 4]), ALU.mult))
            link(v.tensor_reduce(le, pv.rearrange("p t g e -> p t e g"), AX.X, ALU.add))
            link(v.tensor_reduce(m1, le, AX.X, ALU.max))
            link(v.tensor_tensor(ld, le, b4(m1), ALU.subtract))
            first_of(ld, lc, n1, oh1)
            link(v.scalar_tensor_tensor(out=le2, in0=oh1, scalar=-1e30, in1=le, op0=ALU.mult, op1=ALU.add))
            link(v.tensor_reduce(m2, le2, AX.X, ALU.max))
            v.tensor_tensor(t1, m2, m1, ALU.subtract).then_inc(r_dve, 1)
            link(v.tensor_tensor(le2, le2, b4(m2), ALU.subtract))
            first_of(le2, lc2, n2, oh2)
            for o, ohx in ((a1, oh1), (a2, oh2)):
                ins = v.tensor_tensor(o.rearrange("p t (g e) -> p t g e", g=4),
                                      gsel.unsqueeze(3).to_broadcast([P, 3, 4, 4]),
                                      ohx.unsqueeze(2).to_broadcast([P, 3, 4, 4]), ALU.mult)
            link(ins)
            v.tensor_tensor(a12, a1, a2, ALU.add).then_inc(assigned, 1)
            dve.wait_ge(r_act, 1)
            link(v.tensor_reduce(gsum, gexp, AX.X, ALU.add))
            dve.wait_ge(r_act, 2)
            link(v.tensor_scalar(w2, e2, 1.0, None, ALU.add))
            link(v.tensor_tensor(gsum, gsum, w2, ALU.mult))
            link(v.reciprocal(w1, gsum))
            link(v.tensor_tensor(w2, w1, e2, ALU.mult))
            dve.wait_ge(pos_psum, 1)
            v.tensor_copy(pos[:, 0:2, :], ps[:, 6, 0:32].rearrange("p (t n) -> p t n", t=2))
            v.tensor_copy(pos[0:NSM, 2, :], ps[0:NSM, 6, 32:48])
            link(v.tensor_copy(tot, ps[:, 6, 48:64]))
            for ax, psx, qx, nx, gsx in ((a1, ps1, q1, n1, gs1), (a2, ps2, q2, n2, gs2)):
                link(v.tensor_tensor(prod16, ax, pos, ALU.mult))
                link(v.tensor_reduce(psx, prod16, AX.X, ALU.add))
                link(v.tensor_scalar(qx, psx, float(CAP), None, ALU.is_ge))
                for r in range(2, MAXQ):
                    link(v.scalar_tensor_tensor(out=qx, in0=psx, scalar=float(CAP * r), in1=qx, op0=ALU.is_ge,
                                                op1=ALU.add))
                link(v.tensor_scalar(gsx, nx, float(CAP), float(8 * CAP + 32 * CAP), ALU.mult, ALU.add))
                link(v.scalar_tensor_tensor(out=gsx, in0=gmin, scalar=float(4 * CAP), in1=gsx, op0=ALU.mult, op1=ALU.add))
                link(v.scalar_tensor_tensor(out=gsx, in0=qx, scalar=float(NE * CAP - CAP), in1=gsx, op0=ALU.mult,
                                            op1=ALU.add))
                link(v.tensor_tensor(gsx, gsx, psx, ALU.add))
            link(v.tensor_reduce(mc, tot, AX.X, ALU.max))
            link(v.tensor_scalar(nr, mc, float(CAP), None, ALU.is_gt))
            for r in range(2, MAXQ):
                link(v.scalar_tensor_tensor(out=nr, in0=mc, scalar=float(CAP * r), in1=nr, op0=ALU.is_gt, op1=ALU.add))
            v.tensor_scalar(nsteps[:, 0:1], nr, float(PAIRS), float(PAIRS), ALU.mult, ALU.add)
            v.tensor_scalar(nsteps[:, 1:2], nr, float(PAIRS), float(PAIRS + 1), ALU.mult, ALU.add).then_inc(routes, 1)

            def make_sel():
                for t in range(3):
                    ins = v.tensor_scalar(sel[:, t, :], iota_s, gs1[:, t, :], None, ALU.is_equal)
                return ins

            def add_sel():
                for t in range(3):
                    ins = v.scalar_tensor_tensor(out=sel[:, t, :], in0=iota_s, scalar=gs2[:, t, :], in1=sel[:, t, :],
                                                 op0=ALU.is_equal, op1=ALU.add)
                return ins

            dve.wait_ge(m_out_ready, KD)
            link(make_sel())
            add_sel().then_inc(sel_ready, 1)
            dve.wait_ge(utok_psum, 3)
            v.tensor_copy(utok[0:NSM, 2, :].rearrange("p (b n) -> p b n", b=2), ps[0:NSM, 4:6, :])\
                .then_inc(utok_ready, 1)
            dve.sem_inc(sc_added[0], 1)
            dve.sem_inc(sc_added[1], 1)
            dve.sem_inc(selt_ready, 1)
            dve.wait_ge(routes, 1)
            end = dve.value_load(nsteps[0:1, 1:2], min_val=PAIRS + 1, max_val=PAIRS * MAXQ + 1)
            steps = dve.value_load(nsteps[0:1, 0:1], min_val=PAIRS, max_val=PAIRS * MAXQ)
            with dve.Fori(1, end) as step:
                for t in range(3):
                    v.tensor_scalar(selw[:, t, :], iota_s, gs1[:, t, :], w1[:, t, :], ALU.is_equal, ALU.mult)
                    ins = v.tensor_scalar(seltmp[:, t, :], iota_s, gs2[:, t, :], w2[:, t, :], ALU.is_equal, ALU.mult)
                ins.then_inc(selw_parts, 1)
                dve.wait_ge(selw_parts, step)
                v.tensor_tensor(selw, selw, seltmp, ALU.add).then_inc(selw_ready, 1)
                v.tensor_scalar(gs1, gs1, -2.0 * CAP, None, ALU.add)
                v.tensor_scalar(gs2, gs2, -2.0 * CAP, None, ALU.add).then_inc(gs_moved, 1)
                dve.wait_ge(gs_moved, step)
                dve.wait_ge(xg_psum, step)
                make_sel().then_inc(sel_half, 1)
                dve.wait_ge(sel_half, step)
                add_sel().then_inc(sel_ready, 1)
                dve.wait_ge(silu_ready, step)
                dve.wait_ge(up_done, step)
                v.tensor_tensor(hid, silu_e, ps[:, 1, :], ALU.mult).then_inc(hid_ready, 1)
                dve.wait_ge(selt_psum, step)
                v.tensor_copy(selt, ps[:, 0, 0:T]).then_inc(selt_ready, 1)
                for c in range(KD):
                    dve.wait_ge(sc_psum[c % 2], 4 * step - 3 + c // 2)
                    v.tensor_tensor(h[:, c, :], h[:, c, :], ps[:, SC[c % 2], 0:T], ALU.add).then_inc(sc_added[c % 2], 1)
            dve.wait_ge(sc_added[0], 4 * steps + 1)
            dve.wait_ge(sc_added[1], 4 * steps + 1)
            normed(u, "g_ple", 3, u_ready)
            for j in range(KD):
                dve.wait_ge(gate_sig, j + 1)
                v.tensor_tensor(sg[:, j % 2, :], sg[:, j % 2, :], ps[:, 2 + j % 2, 0:T], ALU.mult).then_inc(gate_mul, 1)
                dve.wait_ge(gate_mul, j + 1)
                v.tensor_tensor(h[:, j, :], h[:, j, :], sg[:, j % 2, :], ALU.add).then_inc(h_ple, 1)
            dve.wait_ge(h_ple, KD)
            normed(yo, "g_final", 4, yo_ready)


def _layout(x):
    f = lambda a: np.asarray(a)

    def feat(a, n):
        a = f(a)
        return np.moveaxis(a.reshape(a.shape[:-1] + (n, P)), (-1, -2), (0, 1))

    def slots(w, k, n):
        w = f(w)
        return w.reshape(k, P, w.shape[1] // n, n).transpose(2, 1, 0, 3).reshape(-1, P, k * n)

    w_in = f(x["w_in"])[0]
    glu_cols = w_in[:, :2 * D].reshape(D, 2, KD, P).transpose(0, 2, 1, 3).reshape(D, KD, 256)
    dt = w_in[:, 5 * D:]
    by_kind = {"g": glu_cols, "z": w_in[:, 2 * D:3 * D].reshape(D, 4, 256), "x": w_in[:, 3 * D:5 * D].reshape(D, 8, 256)}
    gu = [f(x[n])[0].reshape(PAIRS, 2, 2, 4, P, FF).transpose(0, 2, 1, 4, 3, 5) for n in ("w_gate_e", "w_up_e")]
    gu = np.stack(gu, axis=1).reshape(PAIRS, 8, P, SLOT)
    down = f(x["w_down_e"])[0].reshape(PAIRS, 2, 2, 2, P, D).transpose(0, 2, 1, 4, 3, 5).reshape(PAIRS, 4, P, SLOT)
    col = lambda a, n: feat(f(a).reshape(-1), n)
    prm = [col(x["g_mix"], 8), col(x["conf_dw_b"], 8), col(x["conf_ln_g"], 8), col(x["conf_ln_b"], 8),
           col(x["ssm_norm_g"], 8), col(x["g_ffn"], 8), col(x["g_ple"], 8), col(x["g_final"], 8),
           col(np.repeat(f(x["d_skip"])[0], HD), 8), col(x["ssm_conv_b"], 16),
           feat(f(x["conf_dw_w"])[0], 8).reshape(P, -1), feat(f(x["ssm_conv_w"])[0], 16).reshape(P, -1)]
    rows = lambda a, b: np.concatenate([f(a).reshape(NPR, -1), f(b).reshape(NSM, -1)], axis=0)
    ar = {
        "xT": feat(rows(x["x_prompt"], x["x_sample"]), KD),
        "pT": feat(rows(x["p_prompt"], x["p_sample"]), 2),
        "w_in": slots(np.concatenate([by_kind[kind][:, i] for kind, i in W_IN_ORDER], axis=1), KD, 256),
        "w_dt": f(dt).reshape(KD, P, NH).transpose(1, 0, 2),
        "w_out": slots(f(x["w_out"])[0], 16, P),
        "w_moe": np.concatenate([gu, down], axis=1),
        "w_router": np.concatenate([f(x["w_rg"])[0], f(x["w_re"])[0]], axis=1).reshape(KD, P, 20).transpose(1, 0, 2),
        "b_router": np.broadcast_to(np.concatenate([f(x["b_rg"])[0], f(x["b_re"])[0]]), (P, 20)),
        "w_pleg": slots(f(x["w_ple_gate"])[0], KD, 256),
        "w_ple": slots(f(x["w_ple"])[0], 2, D)[0],
        "params": np.concatenate(prm, axis=1),
        "hparams": np.stack([f(x["dt_bias"])[0], f(x["a_log"])[0]], axis=1),
        "conf_s": feat(f(x["state_conf_conv"])[0].transpose(1, 0, 2), KD),
        "ssm_s": feat(f(x["state_ssm_conv"])[0].transpose(1, 0, 2), NX),
        "state_s": f(x["state_ssm"])[0].reshape(NSM, KD, P, P).transpose(2, 1, 0, 3),
    }
    return {k: np.ascontiguousarray(v) for k, v in ar.items()}


_OUTS = [("yT", (P, KD, T)), ("conf_p_out", (P, KD, KC - 1)), ("ssm_p_out", (P, NX, KS - 1)), ("h_p_out", (P, D)),
         ("conf_s_out", (P, KD, KC - 1, NSM)), ("ssm_s_out", (P, NX, KS - 1, NSM)), ("h_s_out", (P, KD, NSM, P))]


def kernel(**inputs):
    import concourse.bacc as _bacc
    from concourse.bass_utils import run_bass_kernel_spmd as _run

    nc = _bacc.Bacc("TRN2", target_bir_lowering=False, num_devices=1)
    arrays, args = {}, {}
    for name, a in _layout(inputs).items():
        arrays[f"in_{name}"] = a
        args[name] = nc.dram_tensor(f"in_{name}", a.shape, F32, kind="ExternalInput").ap()
    for name, shape in _OUTS:
        args[name] = nc.dram_tensor(f"out_{name}", shape, F32, kind="ExternalOutput").ap()
    build(nc, **args)
    r = _run(nc, [arrays], core_ids=[0]).results[0]
    o = {name: np.asarray(r[f"out_{name}"]) for name, _ in _OUTS}
    y = o["yT"].transpose(2, 1, 0).reshape(T, D)
    return (
        y[:NPR].reshape(1, NPR, D),
        y[NPR:].reshape(NSM, 1, D),
        o["conf_p_out"].transpose(2, 1, 0).reshape(1, 1, KC - 1, D),
        o["ssm_p_out"].transpose(2, 1, 0).reshape(1, 1, KS - 1, NX * P),
        o["h_p_out"].reshape(P, NH, HD).transpose(1, 2, 0).reshape(1, 1, NH, HD, P),
        o["conf_s_out"].transpose(3, 2, 1, 0).reshape(1, NSM, KC - 1, D),
        o["ssm_s_out"].transpose(3, 2, 1, 0).reshape(1, NSM, KS - 1, NX * P),
        o["h_s_out"].transpose(2, 1, 0, 3).reshape(1, NSM, NH, HD, P),
    )
```

```python
from contextlib import ExitStack

import numpy as np

import concourse.bass as bass
from concourse import mybir

ALU = mybir.AluOpType
ACT = mybir.ActivationFunctionType
AX = mybir.AxisListType
F32 = mybir.dt.float32
I32 = mybir.dt.int32

P = 128
D = 1024
KD = D // P
NPR = 256
NSM = 8
T = NPR + NSM
KC = 31
KS = 4
NH = 16
HD = 64
NG = 4
NX = 16
Q = 128
NE = 16
CAP = 64
MAXQ = -(-T // CAP)
PAIRS = NE // 2
FF = 512
EPS = 1e-6
SLOT = 2048
MIXR = 4
MOER = 12
NWIN = 20
NWOUT = 8
MOE_SLOT = [8, 4, 5, 6, 7, 9, 10, 11, 0, 1, 2, 3]
W_IN_ORDER = [(c[0], int(c[1])) for c in "g0 x0 x1 g1 x2 x3 g2 g3 x4 x5 g4 g5 x6 x7 g6 g7 z0 z1 z2 z3".split()]
NEARLY = 14
AFTER_ITEM = [range(31 + i, 32 + i) for i in range(6)] + [range(37, 39), range(39, 40)]
Z_SILU = 37
POOL_CONV = 3
NORM_BANK = [None, 4, 0, 4, 5]
AT = {ki: n for n, ki in enumerate(W_IN_ORDER)}
TOK = [(0, 128), (128, 128), (256, 8)]

PRM = {}
_at = 0
for _n, _w in (("g_mix", 8), ("conv_b", 8), ("ln_g", 8), ("ln_b", 8), ("ssm_g", 8), ("g_ffn", 8), ("g_ple", 8),
               ("g_final", 8), ("d_skip", 8), ("xconv_b", 16), ("conv_w", 8 * KC), ("xconv_w", 16 * KS)):
    PRM[_n] = (_at, _w)
    _at += _w
NPRM = _at


def build(nc, xT, pT, w_in, w_dt, w_out, w_moe, w_router, b_router, w_pleg, w_ple, params, hparams,
          conf_s, ssm_s, state_s, yT, conf_p_out, ssm_p_out, h_p_out, conf_s_out, ssm_s_out, h_s_out):
    with ExitStack() as ctx:
        def sb(name, shape, dt=F32):
            return ctx.enter_context(nc.sbuf_tensor(name, shape, dt))

        def sem(name):
            return ctx.enter_context(nc.semaphore(name))

        ring = sb("ring", [P, MOER, SLOT])
        h = sb("h", [P, KD, T])
        u = sb("u", [P, KD, T])
        prm = sb("prm", [P, NPRM])
        ident = sb("ident", [P, P])
        mean_k = sb("mean_k", [P, P])
        mean_g = sb("mean_g", [P, P])
        causal = sb("causal", [P, P])[:, :]
        eps = sb("eps", [P, 1])
        warm = sb("warm", [P, 12])
        glu = sb("glu", [P, KD, KC - 1 + NPR])
        cat = sb("cat", [P, 2 * KD, T])
        xraw = sb("xraw", [P, NX, KS - 1 + NPR])
        xraw_s = sb("xraw_s", [P, NX, KS, NSM])
        xbc = sb("xbc", [P, NX, T])
        btok = sb("btok", [P, 2, NG, P])
        hst = sb("hst", [P, D])
        cbm = sb("cbm", [P, 2, NG, P])
        mexp = sb("mexp", [P, 2, 4, P])
        ea = sb("ea", [P, 4, P])
        prod = sb("prod", [P, 256])
        asg = sb("asg", [P, 2, 2, T])
        cdec = sb("cdec", [P, 4])
        hp = sb("hp", [NH, 2])
        hs = sb("hs", [NH, 6, T])
        htok = sb("htok", [P, 6, NH])
        chd = sb("chd", [P, KD, 16])
        dtx = sb("dtx", [P, KD, NSM])
        wdt = sb("wdt", [P, KD, NH])
        scratch = ring[:, MIXR:MOER, :].rearrange("p a b -> p (a b)")
        state = scratch[:, 0:8192].rearrange("p (j b n) -> p j b n", j=KD, b=NSM)
        outer = scratch[:, 8192:10240].rearrange("p (q b n) -> p q b n", q=2, b=NSM)
        glu_s = scratch[:, 10240:12224].rearrange("p (j k b) -> p j k b", j=KD, k=KC)
        pr_s = xraw_s[:, :, :, :].rearrange("p a b c -> p (a b c)")
        part = outer[:, :, :, :].rearrange("p q b n -> p q (b n)")
        part_sum = scratch[:, 14336:14336 + 4 * NPR]
        zs = scratch[:, 12224:12224 + KD * T].rearrange("p (j n) -> p j n", j=KD)
        cbc = scratch[:, 14336:16384].rearrange("p (q b n) -> p q b n", q=2, b=NSM)
        x0 = xraw[:, :, :].rearrange("p a b -> p (a b)")
        xdt = x0[:, 0:2 * D].rearrange("p (c n) -> p c n", c=2)
        xdec = x0[:, 2 * D:4 * D].rearrange("p (c n) -> p c n", c=2)
        a0 = xbc[:, :, :].rearrange("p a b -> p (a b)")
        utok = a0[:, 0:3 * D].rearrange("p (t n) -> p t n", t=3)
        sel = a0[:, 3072:3456].rearrange("p (t n) -> p t n", t=3)
        selw = a0[:, 3456:3840].rearrange("p (t n) -> p t n", t=3)
        xg = x0[:, 0:1024].rearrange("p (c n) -> p c n", c=KD)
        ysb = x0[:, 1024:2048].rearrange("p (c n) -> p c n", c=KD)
        silu_e = x0[:, 2048:2560]
        hid = x0[:, 2560:3072]
        hidt = x0[:, 3072:3584].rearrange("p (k n) -> p k n", k=4)
        c0 = glu[:, :, :].rearrange("p a b -> p (a b)")
        selt = c0[:, 0:T]
        seltmp = c0[:, 384:768].rearrange("p (t n) -> p t n", t=3)
        iota_s = c0[:, 768:896]
        before = c0[:, 896:1024]
        ones = c0[:, 1024:1152]
        r0 = mexp[:, :, :, :].rearrange("p a b c -> p (a b c)")

        def small(at, n):
            return r0[:, at:at + 3 * n].rearrange("p (t n) -> p t n", t=3)

        logit = small(0, 20)
        gmax, gsum, gval, gmin, m1, m2, n1, n2, e2, w1, w2, gs1, gs2, q1, q2, ps1, ps2, t1 = [
            small(60 + 3 * i, 1) for i in range(18)]
        gd, gexp, gc, gsel, le, ld, lc, oh1, le2, lc2, oh2 = [small(120 + 12 * i, 4) for i in range(11)]
        prod16, a1, a2, a12, pos = [small(260 + 48 * i, 16) for i in range(5)]
        r_pos = 532
        wr = c0[:, 1152:1312].rearrange("p (k n) -> p k n", k=KD)
        br = c0[0:20, 1312:1313]
        logit_f = c0[0:20, 1320:1320 + T]
        tot = r0[:, 510:526]
        mc = r0[:, 526:527]
        nr = r0[:, 527:528]
        iota4 = r0[:, 528:532]
        nsteps = sb("nsteps", [P, 3], I32)
        pt = btok[:, :, :, :].rearrange("p c g n -> p (c g n)")[:, 0:2 * T].rearrange("p (k n) -> p k n", k=2)
        w_ple_k = [hst[:, :], cbm[:, :, :, :].rearrange("p c g n -> p (c g n)")]
        pw = cat[:, 8:16, :]
        sg = a0[:, 0:4 * T].rearrange("p (q n) -> p q n", q=4)
        rs_gate = a0[:, 4 * T:5 * T]
        yo = cat[:, 0:8, :]
        sq2 = x0[:, 0:KD * T].rearrange("p (j n) -> p j n", j=KD)

        ps = ctx.enter_context(nc.psum_tensor("ps", [P, 8, 512], F32))
        XT = [2, 3, 5, 6]
        BC = [4, 7]
        SC = [7, 2, 1]
        SC_N = [3, 3, 2]

        def par(name, i=0, n=None):
            a, w = PRM[name]
            return prm[:, a + i:a + i + (1 if n is None else n)]

        in_x = [sem(f"in_x{i}") for i in range(2)]
        in_prm, in_h, in_dt, in_cs, in_ss, in_st, in_wr, in_p = [sem("in_" + n) for n in
            ("prm", "hparams", "wdt", "conf_s", "ssm_s", "state", "router", "ple")]
        consts = sem("consts")
        mix_loaded = [sem(f"mix_loaded{i}") for i in range(MIXR)]
        sq_ready = sem("sq_ready")
        stat_ready = sem("stat_ready")
        rs_ready = sem("rs_ready")
        u_ready = sem("u_ready")
        proj_ready = sem("proj_ready")
        proj_evac = sem("proj_evac")
        glu_ready = sem("glu_ready")
        dt_ready = sem("dt_ready")
        act_self = sem("act_self")
        dve_self = sem("dve_self")
        pool_self = sem("pool_self")
        conv_done = sem("conv_done")
        conv_s_done = sem("conv_s_done")
        xconv_done = sem("xconv_done")
        xbc_ready = sem("xbc_ready")
        ln_mean = sem("ln_mean")
        ln_xc = sem("ln_xc")
        ln_sq = sem("ln_sq")
        ln_var = sem("ln_var")
        ln_rs = sem("ln_rs")
        ln_n = sem("ln_n")
        a_out_ready = sem("a_out_ready")
        dt_act = sem("dt_act")
        dt_dve = sem("dt_dve")
        hrow_ready = sem("hrow_ready")
        htok_psum = sem("htok_psum")
        htok_ready = sem("htok_ready")
        xtok_psum = sem("xtok_psum")
        xtok_ready = sem("xtok_ready")
        btok_psum = sem("btok_psum")
        btok_ready = sem("btok_ready")
        cb_psum = sem("cb_psum")
        cb_ready = sem("cb_ready")
        bc_psum = sem("bc_psum")
        dif_ready = sem("dif_ready")
        exp_ready = sem("exp_ready")
        ea_ready = sem("ea_ready")
        m_ready = sem("m_ready")
        ce_ready = sem("ce_ready")
        y_psum = sem("y_psum")
        st_ready = sem("st_ready")
        y_ready = sem("y_ready")
        hp_done = sem("hp_done")
        dtx_ready = sem("dtx_ready")
        bbc_psum = sem("bbc_psum")
        cbc_psum = sem("cbc_psum")
        cbc_ready = sem("cbc_ready")
        outer_ready = sem("outer_ready")
        snew_ready = sem("snew_ready")
        ttr_done = sem("ttr_done")
        y_s_ready = sem("y_s_ready")
        ycat_ready = sem("ycat_ready")
        gsq_ready = sem("gsq_ready")
        gstat = sem("gstat")
        grs = sem("grs")
        m_out_ready = sem("m_out_ready")
        out_used = sem("out_used")
        o_psum = sem("o_psum")
        o_added = sem("o_added")
        out_conf_p, out_ssm_p, out_h_p, out_conf_s, out_ssm_s, out_h_s, out_y = [sem("out_" + n) for n in
            ("conf_p", "ssm_p", "h_p", "conf_s", "ssm_s", "h_s", "y")]
        log_psum = sem("log_psum")
        logf_ready = sem("logf_ready")
        logt_psum = sem("logt_psum")
        utok_psum = sem("utok_psum")
        utok_ready = sem("utok_ready")
        utok_last = sem("utok_last")
        r_dve = sem("r_dve")
        r_act = sem("r_act")
        assigned = sem("assigned")
        pos_psum = sem("pos_psum")
        routes = sem("routes")
        sel_ready = sem("sel_ready")
        selw_ready = sem("selw_ready")
        xg_psum = sem("xg_psum")
        xg_ready = sem("xg_ready")
        moe_loaded = [sem(f"moe_loaded{i}") for i in range(MOER)]
        y_done = [sem(f"y_done{o}") for o in range(2)]
        moe_used = [sem(f"moe_used{i}") for i in range(MOER - 1)] + [y_done[1]]
        gate_done, up_done = moe_used[3], moe_used[7]
        silu_ready = sem("silu_ready")
        hid_ready = sem("hid_ready")
        hidt_psum = sem("hidt_psum")
        hidt_ready = sem("hidt_ready")
        selt_psum = sem("selt_psum")
        selt_ready = sem("selt_ready")
        ytok_ready = [sem(f"ytok_ready{o}") for o in range(2)]
        sc_psum = [sem(f"sc_psum{q}") for q in range(3)]
        sc_added = [sem(f"sc_added{q}") for q in range(3)]
        selw_parts = sem("selw_parts")
        part_ready = sem("part_ready")
        part_used = sem("part_used")
        pconv_done = sem("pconv_done")
        z_ready = sem("z_ready")
        g_root = sem("g_root")
        ln_root = sem("ln_root")
        pw_psum = sem("pw_psum")
        pw_ready = sem("pw_ready")
        gs_moved = sem("gs_moved")
        sel_half = sem("sel_half")
        ple_loaded = [sem(f"ple_loaded{i}") for i in range(4)]
        gate_psum = sem("gate_psum")
        gate_scaled = sem("gate_scaled")
        gate_sig = sem("gate_sig")
        gate_mul = sem("gate_mul")
        h_ple = sem("h_ple")
        yo_ready = sem("yo_ready")

        block = ctx.enter_context(nc.Block())

        @block.sync
        def _(sp):
            def read(n):
                if n < NWIN:
                    sp.wait_ge(proj_ready, 2 * n + 2)
                elif n < NWIN + NWOUT // 2:
                    sp.wait_ge(out_used, n - NWIN + 1)
                else:
                    sp.wait_ge(o_psum, 2 * (n - NWIN - NWOUT // 2) + 2)

            for i in range(2):
                sp.dma_start(h[:, 4 * i:4 * i + 4, :], xT[:, 4 * i:4 * i + 4, :]).then_inc(in_x[i], 16)
            for n in range(NWIN + NWOUT):
                if n >= MIXR:
                    read(n - MIXR)
                src = w_in[n] if n < NWIN else w_out[n - NWIN]
                sp.dma_start(ring[:, n % MIXR, :], src).then_inc(mix_loaded[n % MIXR], 16)
            last_user = {n % MIXR: n for n in range(NWIN + NWOUT)}
            for j in range(MOER):
                s = MOE_SLOT[j]
                if s < MIXR:
                    read(last_user[s])
                elif s >= 9:
                    sp.wait_ge(ycat_ready, NG)
                    sp.wait_ge(out_conf_s, 16)
                    sp.wait_ge(y_s_ready, KD)
                elif s == 8:
                    sp.wait_ge(snew_ready, KD)
                else:
                    sp.wait_ge(out_h_s, 16 * KD)
                    sp.wait_ge(y_s_ready, KD)
                sp.dma_start(ring[:, s, :], w_moe[0, j]).then_inc(moe_loaded[j], 16)
            with sp.Fori(1, PAIRS) as pair:
                for j in range(MOER):
                    sp.wait_ge(moe_used[j], pair)
                    sp.dma_start(ring[:, MOE_SLOT[j], :], w_moe[pair, j]).then_inc(moe_loaded[j], 16)
            sp.wait_ge(routes, 1)
            end = sp.value_load(nsteps[0:1, 0:1], min_val=PAIRS, max_val=PAIRS * MAXQ)
            with sp.If(end > PAIRS):
                with sp.Fori(PAIRS, end, PAIRS) as first:
                    with sp.Fori(0, PAIRS) as pair:
                        for j in range(MOER):
                            sp.wait_ge(moe_used[j], first + pair)
                            sp.dma_start(ring[:, MOE_SLOT[j], :], w_moe[pair, j]).then_inc(moe_loaded[j], 16)
            for i in range(4):
                sp.wait_ge(moe_used[i], end)
                sp.dma_start(ring[:, MOE_SLOT[i], :], w_pleg[i]).then_inc(ple_loaded[i], 16)
            for j in range(0, KD, 2):
                sp.wait_ge(yo_ready, j + 2)
                sp.dma_start(yT[:, j:j + 2], yo[:, j:j + 2]).then_inc(out_y, 16)
            sp.wait_ge(out_y, 16 * KD // 2)
            for s, n in ((out_conf_p, 1), (out_ssm_p, 1), (out_h_p, 1), (out_conf_s, 1), (out_ssm_s, 1), (out_h_s, KD)):
                sp.wait_ge(s, 16 * n)

        @block.gpsimd
        def _(pool):
            g = nc.gpsimd
            g.memset(ident[:, :], 0.0)
            g.memset(mean_k[:, :], 1.0 / D)
            g.memset(mean_g[:, :], 1.0 / 256)
            g.memset(causal[:, :], 1.0)
            g.memset(eps[:, :], EPS)
            g.memset(glu[:, :, 0:KC - 1], 0.0)
            g.memset(xraw[:, :, 0:KS - 1], 0.0).then_inc(pool_self, 1)
            pool.wait_ge(pool_self, 1)
            g.affine_select(out=ident[:, :], in_=ident[:, :], compare_op=ALU.not_equal, fill=1.0, base=0,
                            pattern=[[-1, P]], channel_multiplier=1)
            g.affine_select(out=causal[:, :], in_=causal[:, :], compare_op=ALU.is_ge, fill=0.0, base=0,
                            pattern=[[1, P]], channel_multiplier=-1).then_inc(consts, 1)
            pool.dma_start(glu_s[:, :, 0:KC - 1, :], conf_s).then_inc(in_cs, 16)
            pool.dma_start(xraw_s[:, :, 0:KS - 1, :], ssm_s).then_inc(in_ss, 16)
            pool.dma_start(state, state_s).then_inc(in_st, 16)
            def new_states(i):
                pool.wait_ge(outer_ready, i + 1)
                g.tensor_tensor(state[:, i], state[:, i], outer[:, i % 2], ALU.add).then_inc(snew_ready, 1)
                pool.wait_ge(snew_ready, i + 1)
                pool.dma_start(h_s_out[:, i], state[:, i]).then_inc(out_h_s, 16)

            def add_part(q):
                n = min(4, KC - 4 * q) * NPR
                pool.wait_ge(part_ready, q + 1)
                if q > 1:
                    pool.wait_ge(part_used, q - 1)
                g.tensor_tensor(part_sum[:, 0:n], part_sum[:, 0:n], part[:, q % 2, 0:n], ALU.add).then_inc(part_used, 1)

            pool.wait_ge(in_cs, 16)
            for j in range(KD):
                pool.wait_ge(proj_evac, 2 * AT["g", j] + 2)
                g.tensor_tensor(glu[:, j, KC - 1:], asg[:, 0, j % 2, 0:NPR], asg[:, 1, j % 2, 0:NPR], ALU.mult)
                g.tensor_tensor(glu_s[:, j, KC - 1, :], asg[:, 0, j % 2, NPR:T], asg[:, 1, j % 2, NPR:T],
                                ALU.mult).then_inc(glu_ready, 1)
                for q in {POOL_CONV: (1, 2, 3), POOL_CONV + 1: (4,), POOL_CONV + 2: (5, 6, 7)}.get(j, ()):
                    add_part(q)
                if j == POOL_CONV + 2:
                    for n in (2 * NPR, NPR):
                        pool.wait_ge(part_used, 7 + (n == NPR))
                        out = part_sum[:, 0:n] if n > NPR else cat[:, POOL_CONV, 0:NPR]
                        g.tensor_tensor(out, part_sum[:, 0:n], part_sum[:, n:2 * n], ALU.add)\
                            .then_inc(part_used if n > NPR else pconv_done, 1)
                if j == 5:
                    pool.wait_ge(proj_evac, 2 * NEARLY)
                    pool.dma_start(ssm_p_out, xraw[:, :, NPR:]).then_inc(out_ssm_p, 16)
                    pool.wait_ge(in_ss, 16)
                    pool.dma_start(ssm_s_out, xraw_s[:, :, 1:, :]).then_inc(out_ssm_s, 16)
                if j == 6:
                    new_states(0)
                    new_states(1)
            pool.wait_ge(glu_ready, KD)
            pool.dma_start(conf_p_out, glu[:, :, NPR:]).then_inc(out_conf_p, 16)
            pool.dma_start(conf_s_out, glu_s[:, :, 1:, :]).then_inc(out_conf_s, 16)
            for i in range(2, KD):
                new_states(i)
            pool.wait_ge(hp_done, NG)
            pool.dma_start(h_p_out, hst[:, :]).then_inc(out_h_p, 16)
            pool.wait_ge(ln_n, 4)
            pool.wait_ge(out_conf_p, 16)
            pool.dma_start(wr, w_router).then_inc(in_wr, 16)
            pool.dma_start(br, b_router).then_inc(in_wr, 16)
            pool.wait_ge(out_h_p, 16)
            pool.dma_start(pt, pT).then_inc(in_p, 16)
            for k in range(2):
                pool.dma_start(w_ple_k[k], w_ple[k]).then_inc(in_p, 16)
            g.memset(ones, 1.0)
            g.memset(before, 1.0)
            g.memset(r0[:, 0:528], 0.0)
            g.iota(iota_s, [[1, P]], base=0, channel_multiplier=0, allow_small_or_imprecise_dtypes=True)
            g.iota(iota4, [[1, 4]], base=0, channel_multiplier=0, allow_small_or_imprecise_dtypes=True)\
                .then_inc(pool_self, 1)
            pool.wait_ge(pool_self, 2)
            g.affine_select(out=before, in_=before, compare_op=ALU.is_gt, fill=0.0, base=0,
                            pattern=[[1, P]], channel_multiplier=-1).then_inc(consts, 1)

        @block.scalar
        def _(act):
            a = nc.scalar
            n_self = [0]

            def link(ins):
                n_self[0] += 1
                ins.then_inc(act_self, 1)
                act.wait_ge(act_self, n_self[0])

            act.dma_start(prm[:, :], params).then_inc(in_prm, 16)
            act.dma_start(wdt[:, :, :], w_dt).then_inc(in_dt, 16)
            act.dma_start(hp[:, :], hparams).then_inc(in_h, 16)
            n_warm = [0]

            def load_table(func):
                a.activation(warm[:, n_warm[0]:n_warm[0] + 1], eps[:, 0:1], func)
                n_warm[0] += 1

            def square(i, c, out):
                a.activation(out[:, c, :], h[:, c, :], ACT.Square).then_inc(sq_ready, 1)

            def root(i, out=None):
                act.wait_ge(stat_ready, i)
                o = ps[:, NORM_BANK[i], 0:T]
                link(a.activation(o, o, ACT.Ln, bias=eps[:, 0:1]))
                a.activation(o if out is None else out, o, ACT.Exp, scale=-0.5).then_inc(rs_ready, 1)

            act.wait_ge(consts, 1)
            load_table(ACT.Ln)
            for c in range(KD):
                act.wait_ge(in_x[c // 4], 16)
                square(1, c, cat)
            root(1)
            act.wait_ge(dt_ready, 1)
            act.wait_ge(in_h, 16)
            a.activation(hs[:, 0, :], ps[0:NH, 7, 0:T], ACT.Identity, bias=hp[:, 0:1]).then_inc(dt_act, 1)
            act.wait_ge(dt_act, 1)
            a.activation(hs[:, 1, :], hs[:, 0, :], ACT.Abs).then_inc(dt_act, 1)
            act.wait_ge(dt_act, 2)
            a.activation(hs[:, 1, :], hs[:, 1, :], ACT.Exp, scale=-1.0).then_inc(dt_act, 1)
            a.activation(hp[:, 1:2], hp[:, 1:2], ACT.Exp).then_inc(dt_act, 1)
            def evacuate(n):
                kind, i = W_IN_ORDER[n // 2]
                q = n % 2
                bank = n % 4 if n < 2 * NEARLY else n % 2
                if kind == "g" and i >= 2:
                    act.wait_ge(glu_ready, i - 1)
                act.wait_ge(proj_ready, n + 1)
                if kind == "g":
                    ins = a.activation(asg[:, q, i % 2, :], ps[:, bank, 0:T], ACT.Sigmoid if q else ACT.Copy)
                elif kind == "x":
                    a.activation(xraw[:, 2 * i + q, KS - 1:], ps[:, bank, 0:NPR], ACT.Copy)
                    ins = a.activation(xraw_s[:, 2 * i + q, KS - 1, :], ps[:, bank, NPR:T], ACT.Copy)
                else:
                    ins = a.activation(zs[:, 2 * i + q, :], ps[:, bank, 0:T], ACT.Copy if n < Z_SILU else ACT.Silu)
                ins.then_inc(proj_evac, 1)

            def products(q):
                act.wait_ge(glu_ready, POOL_CONV + 1)
                act.wait_ge(in_prm, 16)
                if q >= 3:
                    act.wait_ge(part_used, q - 2)
                for k in range(4 * q, min(4 * q + 4, KC)):
                    dst = part[:, q % 2] if q else part_sum
                    src, w = glu[:, POOL_CONV, k:k + NPR], par("conv_w", POOL_CONV * KC + k)
                    out = dst[:, (k - 4 * q) * NPR:(k - 4 * q + 1) * NPR]
                    if k == 0:
                        ins = a.activation(out, src, ACT.Identity, scale=w, bias=par("conv_b", POOL_CONV))
                    else:
                        ins = a.activation(out, src, ACT.Copy, scale=w)
                ins.then_inc(part_ready, 1)

            act.wait_ge(pool_self, 1)
            batches = {7: (0,), 8: (1, 2), 9: (3,), 10: (4,), 11: (5,), 12: (6, 7)}
            for s in range(NEARLY):
                evacuate(2 * s)
                evacuate(2 * s + 1)
                for q in batches.get(s, ()):
                    products(q)
                if s == 5:
                    act.wait_ge(dt_dve, 1)
                    for c in range(2):
                        a.activation(hs[:, 4, c * Q:(c + 1) * Q], hs[:, 3, c * Q:(c + 1) * Q], ACT.Exp, scale=-1.0,
                                     bias=hs[:, 3, (c + 1) * Q - 1:(c + 1) * Q])
                    a.activation(hs[:, 4, NPR:T], hs[:, 5, NPR:T], ACT.Exp).then_inc(dt_act, 1)

            def exp_of(i):
                act.wait_ge(dif_ready, i + 1)
                a.activation(mexp[:, i % 2, :, :], mexp[:, i % 2, :, :], ACT.Exp).then_inc(exp_ready, 1)

            def exp_carry(i):
                if i > NG:
                    act.wait_ge(y_psum, i)
                a.activation(ea[:, :, :], ps[:, BC[i % 2], :].rearrange("p (r n) -> p r n", r=4), ACT.Exp)\
                    .then_inc(ea_ready, 1)

            def decode(i):
                if i == 0:
                    act.wait_ge(in_st, 16)
                    act.wait_ge(dtx_ready, 1)
                for b in range(NSM):
                    a.activation(state[:, i, b, :], state[:, i, b, :], ACT.Copy, scale=chd[:, i, 8 + b:9 + b])
                act.wait_ge(bbc_psum, i // 2 + 1)
                if i >= 2:
                    act.wait_ge(snew_ready, i - 1)
                for b in range(NSM):
                    ins = a.activation(outer[:, i % 2, b, :], ps[:, 2 + b // 4, (b % 4) * P:(b % 4 + 1) * P], ACT.Copy,
                                       scale=dtx[:, i, b:b + 1])
                ins.then_inc(outer_ready, 1)

            def keep_c(gr):
                act.wait_ge(cbc_psum, gr + 1)
                if gr >= 2:
                    act.wait_ge(y_s_ready, 2 * gr - 2)
                a.activation(cbc[:, gr % 2].rearrange("p (a b) n -> p a (b n)", a=2), ps[:, 2:4, :], ACT.Copy)\
                    .then_inc(cbc_ready, 1)

            for m in range(0, NX, 2):
                act.wait_ge(xconv_done, m // 2 + 1)
                a.activation(xbc[:, m:m + 2, 0:NPR], xbc[:, m:m + 2, 0:NPR], ACT.Silu).then_inc(xbc_ready, 1)
            evacuate(2 * NEARLY)
            evacuate(2 * NEARLY + 1)
            evacuate(2 * NEARLY + 2)
            for c in range(2):
                act.wait_ge(btok_psum, c + 1)
                a.activation(btok[:, c, :, :], ps[:, BC[c], :].rearrange("p (g n) -> p g n", g=NG), ACT.Copy)\
                    .then_inc(btok_ready, 1)
            act.wait_ge(xconv_done, NX // 2 + 1)
            a.activation(xbc[:, :, NPR:T], xbc[:, :, NPR:T], ACT.Silu).then_inc(xbc_ready, 1)
            exp_of(0)
            for i in range(2 * NG):
                if i + 1 < 2 * NG:
                    exp_of(i + 1)
                    if i + 1 >= NG:
                        exp_carry(i + 1)
                if i == 6:
                    act.wait_ge(proj_evac, Z_SILU)
                    z0 = zs[:, 0:Z_SILU - 2 * AT["z", 0], :]
                    a.activation(z0, z0, ACT.Silu).then_inc(z_ready, 1)
                decode(i)
                for n in AFTER_ITEM[i]:
                    evacuate(n)
                if i % 2:
                    keep_c(i // 2)
            load_table(ACT.Ln)
            for gr in range(NG):
                act.wait_ge(ycat_ready, gr + 1)
                a.activation(u[:, 2 * gr:2 * gr + 2, :], cat[:, 8 + 2 * gr:10 + 2 * gr, :], ACT.Square)\
                    .then_inc(gsq_ready, 1)
            for gr in range(NG):
                act.wait_ge(gstat, gr + 1)
                o = ps[:, 3 + gr, 0:T]
                ins = a.activation(o, o, ACT.Ln, bias=eps[:, 0:1])
            link(ins)
            for gr in range(NG):
                o = ps[:, 3 + gr, 0:T]
                a.activation(o, o, ACT.Exp, scale=-0.5).then_inc(g_root, 1)
            act.wait_ge(ln_xc, 1)
            act.wait_ge(out_conf_p, 16)
            a.activation(glu[:, :, 0:T], cat[:, 0:8, :], ACT.Square).then_inc(ln_sq, 1)
            act.wait_ge(ln_var, 1)
            link(a.activation(ps[:, 7, 0:T], ps[:, 7, 0:T], ACT.Ln, bias=eps[:, 0:1]))
            a.activation(ps[:, 7, 0:T], ps[:, 7, 0:T], ACT.Exp, scale=-0.5).then_inc(ln_root, 1)
            load_table(ACT.Silu)
            for j in range(KD):
                act.wait_ge(ln_n, j // 2 + 1)
                a.activation(cat[:, j, :], cat[:, j, :], ACT.Silu, scale=par("ln_g", j), bias=par("ln_b", j))\
                    .then_inc(a_out_ready, 1)
            load_table(ACT.Ln)
            for c in range(KD):
                act.wait_ge(o_added, c + 1)
                square(2, c, sq2)
            root(2)
            act.wait_ge(r_dve, 1)
            a.activation(gexp, gd, ACT.Exp).then_inc(r_act, 1)
            act.wait_ge(r_dve, 2)
            a.activation(e2, t1, ACT.Exp).then_inc(r_act, 1)
            for t in range(2):
                act.wait_ge(utok_psum, t + 1)
                a.activation(utok[:, t, :].rearrange("p (b n) -> p b n", b=2), ps[:, 2 * t:2 * t + 2, :], ACT.Copy)\
                    .then_inc(utok_ready, 1)
            for j in range(KD):
                act.wait_ge(pw_psum, j + 1)
                a.activation(pw[:, j, :], ps[:, 7 * (j % 2), 0:T], ACT.Copy).then_inc(pw_ready, 1)
            load_table(ACT.Silu)
            act.wait_ge(xg_psum, 1)
            a.activation(xg.rearrange("p (b c) n -> p b (c n)", b=2), ps[:, 5:7, :], ACT.Copy).then_inc(xg_ready, 1)
            act.wait_ge(routes, 1)
            end = act.value_load(nsteps[0:1, 1:2], min_val=PAIRS + 1, max_val=PAIRS * MAXQ + 1)
            steps = act.value_load(nsteps[0:1, 0:1], min_val=PAIRS, max_val=PAIRS * MAXQ)
            last_adds = act.value_load(nsteps[0:1, 2:3], min_val=3 * PAIRS - 1, max_val=3 * PAIRS * MAXQ - 1)
            with act.Fori(1, end) as step:
                act.wait_ge(gate_done, step)
                a.activation(silu_e, ps[:, 0, :], ACT.Silu).then_inc(silu_ready, 1)
                act.wait_ge(hidt_psum, step)
                a.activation(hidt, ps[:, 2, :].rearrange("p (k n) -> p k n", k=4), ACT.Copy).then_inc(hidt_ready, 1)
                act.wait_ge(xg_psum, step + 1)
                a.activation(xg.rearrange("p (b c) n -> p b (c n)", b=2), ps[:, 5:7, :], ACT.Copy).then_inc(xg_ready, 1)
                for o in range(2):
                    act.wait_ge(y_done[o], step)
                    a.activation(ysb[:, 4 * o:4 * o + 4].rearrange("p c n -> p (c n)"), ps[:, 3 + o, :], ACT.Copy)\
                        .then_inc(ytok_ready[o], 1)
            load_table(ACT.Ln)
            for c in range(KD):
                act.wait_ge(sc_added[c % 3], (last_adds if c % 3 < 2 else 2 * steps) + c // 3)
                square(3, c, cat)
            root(3, rs_gate)
            load_table(ACT.Sigmoid)
            for j in range(KD):
                act.wait_ge(gate_scaled, j + 1)
                a.activation(sg[:, j % 4, :], sg[:, j % 4, :], ACT.Sigmoid).then_inc(gate_sig, 1)
                if j == KD - 1:
                    load_table(ACT.Ln)
                if j:
                    act.wait_ge(h_ple, j)
                    square(4, j - 1, cat)
            act.wait_ge(h_ple, KD)
            square(4, KD - 1, cat)
            root(4)

        @block.tensor
        def _(pe):
            mm = nc.tensor.matmul
            tr = nc.tensor.transpose

            def mean_of(x, bank, w, n0=0, n=KD):
                for k in range(n):
                    ins = mm(ps[:, bank, 0:T], w[:, :], x[:, n0 + k, 0:T], start=(k == 0), stop=(k == n - 1))
                return ins

            def mean_square(i, x, c):
                pe.wait_ge(sq_ready, KD * (i - 1) + c + 1)
                ins = mm(ps[:, NORM_BANK[i], 0:T], mean_k[:, :], x[:, c, :], start=(c == 0), stop=(c == KD - 1))
                if c == KD - 1:
                    ins.then_inc(stat_ready, 1)

            pe.wait_ge(consts, 1)
            for c in range(KD):
                mean_square(1, cat, c)
            pe.wait_ge(in_dt, 16)
            for k in range(KD):
                pe.wait_ge(u_ready, k + 1)
                ins = mm(ps[0:NH, 7, 0:T], wdt[:, k, :], u[:, k, :], start=(k == 0), stop=(k == KD - 1))
            ins.then_inc(dt_ready, 1)
            def project(n):
                s, q = divmod(n, 2)
                if q == 0:
                    pe.wait_ge(mix_loaded[s % MIXR], 16 * (s // MIXR + 1))
                wv = ring[:, s % MIXR, :].rearrange("p (k n) -> p k n", k=KD)
                if n >= 4:
                    pe.wait_ge(proj_evac, n - 3 if s <= NEARLY else n - 1)
                for k in range(KD):
                    ins = mm(ps[:, n % (4 if s < NEARLY else 2), 0:T], wv[:, k, q * P:(q + 1) * P], u[:, k, :],
                             start=(k == 0), stop=(k == KD - 1))
                ins.then_inc(proj_ready, 1)

            def spread(i):
                c, gr = divmod(i, NG)
                if i < 2:
                    pe.wait_ge(btok_ready, i + 1)
                else:
                    pe.wait_ge(dif_ready, i - 1)
                    if i - 2 >= NG:
                        pe.wait_ge(ea_ready, i - 2 - NG + 1)
                for r in range(4):
                    hd = 4 * gr + r
                    ins = mm(ps[:, BC[i % 2], r * P:(r + 1) * P], ident[0:NH, hd:hd + 1].to_broadcast([NH, P]),
                             hs[:, 3, c * Q:(c + 1) * Q], start=True, stop=True)
                ins.then_inc(bc_psum, 1)

            def item(i):
                c, gr = divmod(i, NG)
                bank = 5 + i % 2
                pe.wait_ge(m_ready, i + 1)
                if c == 1:
                    pe.wait_ge(ce_ready, gr + 1)
                if i >= 2:
                    pe.wait_ge(y_ready, i - 1)
                else:
                    pe.wait_ge(cb_ready, i + 1)
                for r in range(4):
                    hd = 4 * gr + r
                    q = (r % 2) * HD
                    o = ps[q:q + HD, bank, (r // 2) * P:(r // 2 + 1) * P]
                    mm(o, xdt[:, c, hd * HD:(hd + 1) * HD], mexp[:, i % 2, r, :], start=True, stop=(c == 0))
                    if c == 1:
                        mm(o, hst[:, hd * HD:(hd + 1) * HD], ea[:, r, :], start=False, stop=True)
                mm(ps[:, bank, 256:512], btok[:, c, gr, :], xdec[:, c, gr * 256:(gr + 1) * 256],
                   start=True, stop=True).then_inc(y_psum, 1)

            def spread_rows(m, gr, out_sem):
                if m == 12:
                    pe.wait_ge(outer_ready, 2 * gr + 2)
                elif gr:
                    pe.wait_ge(cbc_ready, gr)
                else:
                    pe.wait_ge(xtok_ready, 4)
                    pe.wait_ge(xbc_ready, NX // 2 + 1)
                for b in range(NSM):
                    ins = mm(ps[:, 2 + b // 4, (b % 4) * P:(b % 4 + 1) * P],
                             xbc[:, m + gr, NPR + b:NPR + b + 1].to_broadcast([P, P]), ident[:, :], start=True, stop=True)
                ins.then_inc(out_sem, 1)

            for n in range(2 * NEARLY):
                project(n)
            pe.wait_ge(hrow_ready, 1)
            for v, row in enumerate((2, 1, 0)):
                for c in range(2):
                    ins = tr(ps[:, 7, (2 * v + c) * NH:(2 * v + c + 1) * NH], hs[:, row, c * Q:(c + 1) * Q],
                             ident[0:NH, 0:NH])
            for hd in range(NH):
                j, q = hd // 2, HD * (hd % 2)
                ins = mm(ps[q:q + HD, 7, P + 16 * j:P + 16 * j + 16], ident[0:NH, hd:hd + 1].to_broadcast([NH, HD]),
                         hs[:, 2:6:2, NPR:T], start=True, stop=True)
            ins.then_inc(htok_psum, 1)
            project(2 * NEARLY)
            project(2 * NEARLY + 1)
            pe.wait_ge(proj_evac, 2 * NEARLY)
            for c in range(2):
                if c == 1:
                    pe.wait_ge(xconv_done, NX // 2)
                for hf in range(2):
                    for j in range(4):
                        if c == 0:
                            pe.wait_ge(xbc_ready, (4 * hf + j) // 2 + 1)
                        ins = tr(ps[:, XT[2 * c + hf], j * P:(j + 1) * P], xbc[:, 4 * hf + j, c * Q:(c + 1) * Q],
                                 ident[:, :])
                    ins.then_inc(xtok_psum, 1)
            project(2 * NEARLY + 2)
            pe.wait_ge(xbc_ready, NX // 2)
            for c in range(2):
                if c == 1:
                    pe.wait_ge(htok_ready, 1)
                for gr in range(NG):
                    ins = tr(ps[:, BC[c], gr * P:(gr + 1) * P], xbc[:, 8 + gr, c * Q:(c + 1) * Q], ident[:, :])
                ins.then_inc(btok_psum, 1)
            for c in range(2):
                pe.wait_ge(xtok_ready, 3 + c)
                for gr in range(NG):
                    ins = mm(ps[:, 5 + c, gr * P:(gr + 1) * P], xbc[:, 8 + gr, c * Q:(c + 1) * Q],
                             xbc[:, 12 + gr, c * Q:(c + 1) * Q], start=True, stop=True)
                ins.then_inc(cb_psum, 1)
            spread(0)
            spread(1)
            for i in range(2 * NG):
                item(i)
                if i + 2 < 2 * NG:
                    spread(i + 2)
                if i % 2 == 0:
                    spread_rows(8, i // 2, bbc_psum)
                for n in AFTER_ITEM[i]:
                    project(n)
                if i % 2:
                    spread_rows(12, i // 2, cbc_psum)
            pe.wait_ge(conv_done, KD - 1)
            pe.wait_ge(pconv_done, 1)
            pe.wait_ge(conv_s_done, KD)
            pe.wait_ge(ea_ready, NG)
            pe.wait_ge(dif_ready, 2 * NG)
            mean_of(cat, 7, mean_k).then_inc(ln_mean, 1)
            pe.wait_ge(cbc_ready, NG)
            pe.wait_ge(y_ready, 2 * NG)
            pe.wait_ge(hp_done, NG)
            for gr in range(NG):
                pe.wait_ge(gsq_ready, gr + 1)
                mean_of(u, 3 + gr, mean_g, n0=2 * gr, n=2).then_inc(gstat, 1)

            def w_out_half(n, hf):
                s = NWIN + 4 * hf + n // 2
                pe.wait_ge(mix_loaded[s % MIXR], 16 * (s // MIXR + 1))
                wv = ring[:, s % MIXR, :].rearrange("p (k n) -> p k n", k=KD)
                for k in range(KD):
                    if n == 0:
                        pe.wait_ge(a_out_ready if hf else m_out_ready, k + 1)
                    ins = mm(ps[:, n, 0:T], wv[:, k, (n % 2) * P:(n % 2 + 1) * P], cat[:, 8 * (1 - hf) + k, :],
                             start=(hf == 0 and k == 0), stop=(hf == 1 and k == KD - 1))
                    if k == KD - 1 and n % 2 and hf == 0:
                        ins.then_inc(out_used, 1)
                return ins

            pe.wait_ge(proj_evac, 2 * NWIN)
            for n in range(KD):
                if n == KD - 1:
                    pe.wait_ge(ln_n, 4)
                w_out_half(n, 0)
                if n == 2:
                    pe.wait_ge(ln_sq, 1)
                    mean_of(glu, 7, mean_k).then_inc(ln_var, 1)
            for n in range(KD + 2):
                if n < KD:
                    w_out_half(n, 1).then_inc(o_psum, 1)
                if n >= 2:
                    mean_square(2, sq2, n - 2)
            pe.wait_ge(in_wr, 32)
            for k in range(KD):
                pe.wait_ge(u_ready, KD + k + 1)
                ins = mm(ps[0:20, 7, 0:T], wr[:, k, :], u[:, k, :], start=(k == 0), stop=(k == KD - 1))
            ins.then_inc(log_psum, 1)
            pe.wait_ge(logf_ready, 1)
            for t, (t0, tn) in enumerate(TOK):
                ins = tr(ps[0:tn, 6, 64 + 20 * t:84 + 20 * t], logit_f[:, t0:t0 + tn], ident[0:20, 0:20])
            ins.then_inc(logt_psum, 1)
            for t, (t0, tn) in enumerate(TOK):
                if t == 2:
                    pe.wait_ge(u_ready, 2 * KD)
                for j in range(KD):
                    ins = tr(ps[0:tn, 2 * t + j // 4, (j % 4) * P:(j % 4 + 1) * P], u[:, j, t0:t0 + tn], ident[:, :])
                ins.then_inc(utok_psum, 1)
            pe.wait_ge(assigned, 1)
            pe.wait_ge(consts, 2)
            for t, (t0, tn) in enumerate(TOK):
                for v in range(t + 1):
                    vn = TOK[v][1]
                    ins = mm(ps[0:tn, 6, 16 * t:16 * t + 16], (before if v == t else ones)[0:vn, 0:tn],
                             a12[0:vn, v, :], start=(v == 0), stop=(v == t))
            for v, (_, vn) in enumerate(TOK):
                ins = mm(ps[:, 6, 48:64], ones[0:vn, :], a12[0:vn, v, :], start=(v == 0), stop=(v == 2))
            ins.then_inc(pos_psum, 1)

            def gather(c0, c1):
                for c in range(c0, c1):
                    for t, (_, tn) in enumerate(TOK):
                        ins = mm(ps[:, 5 + c // 4, (c % 4) * P:(c % 4 + 1) * P], utok[0:tn, t, c * P:(c + 1) * P],
                                 sel[0:tn, t, :], start=(t == 0), stop=(t == 2))
                if c1 == KD:
                    ins.then_inc(xg_psum, 1)

            pe.wait_ge(in_p, 16 * 3)
            pe.wait_ge(assigned, 1)
            pe.wait_ge(utok_ready, 1)
            for j in range(KD):
                if j >= 2:
                    pe.wait_ge(pw_ready, j - 1)
                for k in range(2):
                    ins = mm(ps[:, 7 * (j % 2), 0:T], w_ple_k[k][:, j * P:(j + 1) * P], pt[:, k, :], start=(k == 0),
                             stop=(k == 1))
                ins.then_inc(pw_psum, 1)
            pe.wait_ge(utok_ready, 2)
            pe.wait_ge(utok_last, 1)
            pe.wait_ge(sel_ready, 1)
            gather(0, KD)
            pe.wait_ge(routes, 1)
            end = pe.value_load(nsteps[0:1, 1:2], min_val=PAIRS + 1, max_val=PAIRS * MAXQ + 1)
            steps = pe.value_load(nsteps[0:1, 0:1], min_val=PAIRS, max_val=PAIRS * MAXQ)
            with pe.Fori(1, end) as step:
                pe.wait_ge(xg_ready, step)
                pe.wait_ge(pw_ready, KD)
                pe.wait_ge(selt_ready, step)
                for gu in range(2):
                    if gu == 1:
                        pe.wait_ge(sc_added[2], 2 * step - 1)
                    for hf in range(2):
                        for k in range(4):
                            for e in range(2):
                                j = 4 * gu + 2 * hf + e
                                if k == 0:
                                    pe.wait_ge(moe_loaded[j], 16 * step)
                                wv = ring[:, MOE_SLOT[j], :].rearrange("p (k n) -> p k n", k=4)
                                ins = mm(ps[e * CAP:(e + 1) * CAP, gu, :], xg[:, 4 * hf + k, e * CAP:(e + 1) * CAP],
                                         wv[:, k, :], start=(hf == 0 and k == 0), stop=(hf == 1 and k == 3))
                                if k == 3:
                                    ins.then_inc(moe_used[j], 1)
                pe.wait_ge(selw_ready, step)
                pe.wait_ge(silu_ready, step)
                for t, (t0, tn) in enumerate(TOK):
                    ins = tr(ps[:, 0, t0:t0 + tn], selw[0:tn, t, :], ident[0:tn, 0:tn])
                ins.then_inc(selt_psum, 1)
                pe.wait_ge(sel_ready, step + 1)
                gather(0, 1)
                pe.wait_ge(hid_ready, step)
                pe.wait_ge(sc_added[1], 3 * step - 2)
                for k in range(4):
                    ins = tr(ps[:, 2, k * P:(k + 1) * P], hid[:, k * P:(k + 1) * P], ident[:, :])
                ins.then_inc(hidt_psum, 1)
                gather(1, KD)
                pe.wait_ge(hidt_ready, step)
                for hf in range(2):
                    for k in range(2):
                        for o in range(2):
                            for e in range(2):
                                j = 8 + 2 * hf + e
                                if k == 0 and o == 0:
                                    pe.wait_ge(moe_loaded[j], 16 * step)
                                wv = ring[:, MOE_SLOT[j], :].rearrange("p (k n) -> p k n", k=2)
                                ins = mm(ps[e * CAP:(e + 1) * CAP, 3 + o, :], hidt[:, 2 * hf + k, e * CAP:(e + 1) * CAP],
                                         wv[:, k, o * 512:(o + 1) * 512], start=(hf == 0 and k == 0),
                                         stop=(hf == 1 and k == 1))
                                if k == 1 and o == 1:
                                    ins.then_inc(moe_used[j], 1)
                                elif k == 1 and hf == 1 and e == 1:
                                    ins.then_inc(y_done[0], 1)
                pe.wait_ge(selt_ready, step + 1)
                for c in range(KD):
                    q = c % 3
                    if c % 4 == 0:
                        pe.wait_ge(ytok_ready[c // 4], step)
                    pe.wait_ge(sc_added[q], SC_N[q] * step - SC_N[q] + 1 + c // 3)
                    mm(ps[:, SC[q], 0:T], ysb[:, c, :], selt, start=True, stop=True).then_inc(sc_psum[q], 1)
            pe.wait_ge(ytok_ready[1], steps)
            for q in range(3):
                pe.wait_ge(sc_added[q], SC_N[q] * steps + 1)
            for j in range(KD):
                pe.wait_ge(ple_loaded[j // 2], 16)
                if j >= 4:
                    pe.wait_ge(gate_scaled, j - 3)
                wv = ring[:, MOE_SLOT[j // 2], :].rearrange("p (k n) -> p k n", k=KD)
                for k in range(KD):
                    pe.wait_ge(u_ready, 2 * KD + k + 1)
                    ins = mm(ps[:, j % 4, 0:T], wv[:, k, (j % 2) * P:(j % 2 + 1) * P], u[:, k, :],
                             start=(k == 0), stop=(k == KD - 1))
                ins.then_inc(gate_psum, 1)
                if j == 0:
                    for c in range(KD):
                        mean_square(3, cat, c)
                if j >= 3:
                    mean_square(4, cat, j - 3)
            for c in range(KD - 3, KD):
                mean_square(4, cat, c)

        @block.vector
        def _(dve):
            v = nc.vector
            n_self = [0]

            def link(ins):
                n_self[0] += 1
                ins.then_inc(dve_self, 1)
                dve.wait_ge(dve_self, n_self[0])

            def mark(ins):
                n_self[0] += 1
                ins.then_inc(dve_self, 1)
                return n_self[0]

            def normed(out, gain, i, out_sem):
                rs = ps[:, NORM_BANK[i], 0:T]
                dve.wait_ge(rs_ready, i)
                for j in range(KD):
                    v.scalar_tensor_tensor(out=out[:, j, :], in0=h[:, j, :], scalar=par(gain, j), in1=rs,
                                           op0=ALU.mult, op1=ALU.mult).then_inc(out_sem, 1)

            dve.wait_ge(in_prm, 16)
            dve.wait_ge(in_x[0], 16)
            dve.wait_ge(in_x[1], 16)
            normed(u, "g_mix", 1, u_ready)
            X, E, DT, ACS, DEC, A = range(6)
            dve.wait_ge(dt_act, 4)
            link(v.tensor_scalar(hs[:, A, :], hs[:, E, :], 2.0, None, ALU.add))
            link(v.reciprocal(hs[:, A, :], hs[:, A, :]))
            link(v.tensor_tensor(hs[:, E, :], hs[:, E, :], hs[:, A, :], ALU.mult))
            link(v.tensor_tensor(hs[:, A, :], hs[:, E, :], hs[:, E, :], ALU.mult))
            link(v.tensor_scalar(hs[:, DT, :], hs[:, A, :], 1.0 / 17, None, ALU.mult))
            for k in range(15, 1, -2):
                link(v.scalar_tensor_tensor(out=hs[:, DT, :], in0=hs[:, DT, :], scalar=1.0 / k, in1=hs[:, A, :],
                                            op0=ALU.add, op1=ALU.mult))
            link(v.scalar_tensor_tensor(out=hs[:, DT, :], in0=hs[:, DT, :], scalar=1.0, in1=hs[:, E, :],
                                        op0=ALU.add, op1=ALU.mult))
            link(v.tensor_scalar(hs[:, X, :], hs[:, X, :], 0.0, None, ALU.max))
            link(v.scalar_tensor_tensor(out=hs[:, DT, :], in0=hs[:, DT, :], scalar=2.0, in1=hs[:, X, :],
                                        op0=ALU.mult, op1=ALU.add))
            link(v.tensor_scalar(hs[:, A, :], hs[:, DT, :], hp[:, 1:2], -1.0, ALU.mult, ALU.mult))
            dve.wait_ge(consts, 1)
            link(v.tensor_scalar(hs[:, X, 0:Q], hs[:, A, 0:Q], 0.0, 1.0, ALU.mult, ALU.add))
            for c in range(2):
                ins = v.tensor_tensor_scan(hs[:, ACS, c * Q:(c + 1) * Q], hs[:, X, 0:Q], hs[:, A, c * Q:(c + 1) * Q],
                                           0.0, ALU.mult, ALU.add)
            ins.then_inc(dt_dve, 1)
            dve.wait_ge(dt_dve, 1)
            v.tensor_scalar(hs[:, X, 0:NPR], hs[:, ACS, 0:NPR], -1.0, None, ALU.mult)

            def decode_conv_x():
                dve.wait_ge(in_ss, 16)
                pr = cbm[:, 0, 0:2, :].rearrange("p a (m k b) -> p (a m) k b", m=4, k=KS)
                xw = par("xconv_w", 0, NX * KS).rearrange("p (m k) -> p m k", m=NX)
                for m in (0, 8):
                    link(v.tensor_tensor(pr, xraw_s[:, m:m + 8], xw[:, m:m + 8].unsqueeze(3).to_broadcast([P, 8, KS, NSM]),
                                         ALU.mult))
                    link(v.tensor_reduce(xbc[:, m:m + 8, NPR:T], pr.rearrange("p m k b -> p m b k"), AX.X, ALU.add))
                v.tensor_tensor(xbc[:, :, NPR:T], xbc[:, :, NPR:T],
                                par("xconv_b", 0, NX).unsqueeze(2).to_broadcast([P, NX, NSM]), ALU.add)\
                    .then_inc(xconv_done, 1)

            cw = par("conv_w", 0, KD * KC)

            def decode_conv(j):
                dve.wait_ge(glu_ready, j + 1)
                pr = pr_s[:, 0:KC * NSM].rearrange("p (k b) -> p k b", k=KC)
                link(v.tensor_tensor(pr, glu_s[:, j], cw[:, j * KC:(j + 1) * KC].unsqueeze(2).to_broadcast([P, KC, NSM]),
                                     ALU.mult))
                link(v.tensor_reduce(cat[:, j, NPR:T], pr.rearrange("p k b -> p b k"), AX.X, ALU.add))
                v.tensor_scalar(cat[:, j, NPR:T], cat[:, j, NPR:T], par("conv_b", j), None, ALU.add)\
                    .then_inc(conv_s_done, 1)

            def conv_x(m):
                dve.wait_ge(proj_evac, 2 * AT["x", m // 2] + 2)
                if m:
                    dve.wait_ge(xconv_done, m // 2)
                at = [0, 0]
                for k in range(KS):
                    for q in range(2):
                        src, w = xraw[:, m + q, k:k + NPR], par("xconv_w", (m + q) * KS + k)
                        acc = ps[:, 5 + q, 0:NPR]
                        if k == 0:
                            at[q] = mark(v.tensor_scalar(acc, src, w, par("xconv_b", m + q), ALU.mult, ALU.add))
                            continue
                        dve.wait_ge(dve_self, at[q])
                        ins = v.scalar_tensor_tensor(out=xbc[:, m + q, 0:NPR] if k == KS - 1 else acc, in0=src,
                                                     scalar=w, in1=acc, op0=ALU.mult, op1=ALU.add)
                        if k < KS - 1:
                            at[q] = mark(ins)
                ins.then_inc(xconv_done, 1)

            at_tap = [0, 0]

            def conv(j, k0, k1):
                if k0 == 0:
                    dve.wait_ge(glu_ready, j + 1)
                    if j:
                        dve.wait_ge(conv_done, j - (j > POOL_CONV))
                for k in range(k0, k1):
                    src, w, q = glu[:, j, k:k + NPR], par("conv_w", j * KC + k), k % 2
                    acc = prod[:, :] if q else cat[:, j, 0:NPR]
                    if k < 2:
                        ins = v.tensor_scalar(acc, src, w, None if q else par("conv_b", j), ALU.mult,
                                              *(() if q else (ALU.add,)))
                    else:
                        dve.wait_ge(dve_self, at_tap[q])
                        ins = v.scalar_tensor_tensor(out=acc, in0=src, scalar=w, in1=acc, op0=ALU.mult, op1=ALU.add)
                    at_tap[q] = mark(ins)
                if k1 == KC:
                    dve.wait_ge(dve_self, at_tap[0])
                    v.tensor_tensor(cat[:, j, 0:NPR], cat[:, j, 0:NPR], prod[:, :], ALU.add).then_inc(conv_done, 1)

            for q, j in enumerate((0, 1, 2, 4)):
                if j == 4:
                    dve.wait_ge(dt_act, 5)
                    v.tensor_tensor(hs[:, E, 0:NPR], hs[:, DT, 0:NPR], hs[:, DEC, 0:NPR], ALU.mult).then_inc(hrow_ready, 1)
                conv(j, 0, KC)
                if j == 4:
                    conv(5, 0, 16)
                conv_x(4 * q)
                conv_x(4 * q + 2)
            conv(5, 16, KC)
            decode_conv_x()
            dve.wait_ge(htok_psum, 1)
            v.tensor_copy(chd[:, :, :], ps[:, 7, P:2 * P].rearrange("p (j n) -> p j n", j=KD))
            v.tensor_copy(htok[:, :, :], ps[:, 7, 0:6 * NH].rearrange("p (v n) -> p v n", v=6)).then_inc(htok_ready, 1)
            dve.wait_ge(htok_ready, 1)
            dve.wait_ge(out_ssm_p, 16)
            dve.wait_ge(xconv_done, NX // 2 + 1)
            for i in range(4):
                c, hf = divmod(i, 2)
                dve.wait_ge(xtok_psum, i + 1)
                src = ps[:, XT[i], :].rearrange("p (h d) -> p h d", h=8)
                for dst, row in ((xdt, c), (xdec, 2 + c)):
                    ins = v.tensor_tensor(dst[:, c, hf * 512:(hf + 1) * 512].rearrange("p (h d) -> p h d", h=8), src,
                                          htok[:, row, hf * 8:hf * 8 + 8].unsqueeze(2).to_broadcast([P, 8, HD]), ALU.mult)
                ins.then_inc(xtok_ready, 1)
            for c in range(2):
                dve.wait_ge(cb_psum, c + 1)
                v.tensor_tensor(cbm[:, c, :, :], ps[:, 5 + c, :].rearrange("p (g n) -> p g n", g=NG),
                                causal.unsqueeze(1).to_broadcast([P, NG, P]), ALU.mult).then_inc(cb_ready, 1)
            dve.wait_ge(cb_ready, 2)

            def spread_done(i):
                c, gr = divmod(i, NG)
                dve.wait_ge(exp_ready, i + 1)
                v.tensor_tensor(mexp[:, i % 2, :, :], mexp[:, i % 2, :, :],
                                cbm[:, c, gr, :].unsqueeze(1).to_broadcast([P, 4, P]), ALU.mult).then_inc(m_ready, 1)
                if c == 1:
                    dve.wait_ge(ea_ready, gr + 1)
                    link(v.tensor_copy(cdec[:, :], ea[:, :, P - 1]))
                    v.tensor_tensor(ea[:, :, :], ea[:, :, :],
                                    xbc[:, 12 + gr, Q:2 * Q].unsqueeze(1).to_broadcast([P, 4, P]), ALU.mult)\
                        .then_inc(ce_ready, 1)

            def take(i):
                c, gr = divmod(i, NG)
                bank = 5 + i % 2
                dve.wait_ge(y_psum, i + 1)
                cols = slice(gr * 256, (gr + 1) * 256)
                if c == 0:
                    v.tensor_copy(hst[:, cols], ps[:, bank, 256:512]).then_inc(st_ready, 1)
                else:
                    hv = hst[:, cols].rearrange("p (r d) -> p r d", r=4)
                    link(v.tensor_tensor(hv, hv, cdec[:, :].unsqueeze(2).to_broadcast([P, 4, HD]), ALU.mult))
                    v.tensor_tensor(hst[:, cols], hst[:, cols], ps[:, bank, 256:512], ALU.add).then_inc(hp_done, 1)
                for jj in range(2):
                    j = 2 * gr + jj
                    ins = v.scalar_tensor_tensor(out=cat[:, 8 + j, c * Q:(c + 1) * Q], in0=xbc[:, j, c * Q:(c + 1) * Q],
                                                 scalar=par("d_skip", j), in1=ps[:, bank, jj * P:(jj + 1) * P],
                                                 op0=ALU.mult, op1=ALU.add)
                ins.then_inc(y_ready, 1)

            def difference(i):
                c, gr = divmod(i, NG)
                dve.wait_ge(bc_psum, i + 1)
                if i >= 2:
                    dve.wait_ge(y_psum, i - 1)
                for r in range(4):
                    hd = 4 * gr + r
                    ins = v.tensor_scalar(mexp[:, i % 2, r, :], ps[:, BC[i % 2], r * P:(r + 1) * P],
                                          htok[:, 4 + c, hd:hd + 1], 0.0, ALU.add, ALU.min)
                ins.then_inc(dif_ready, 1)

            def decode(i):
                dve.wait_ge(snew_ready, i + 1)
                dve.wait_ge(cbc_ready, i // 2 + 1)
                for b in range(NSM):
                    if b > 1:
                        dve.wait_ge(ttr_done, NSM * i + b - 1)
                    v.tensor_tensor_reduce(out=pr_s[:, 256 + P * (b % 2):256 + P * (b % 2 + 1)], in0=state[:, i, b, :],
                                           in1=cbc[:, i // 2 % 2, b, :], scale=1.0, scalar=0.0,
                                           op0=ALU.mult, op1=ALU.add, accum_out=cat[:, 8 + i, NPR + b:NPR + b + 1])\
                        .then_inc(ttr_done, 1)
                dve.wait_ge(ttr_done, NSM * (i + 1))
                v.scalar_tensor_tensor(out=cat[:, 8 + i, NPR:T], in0=xbc[:, i, NPR:T], scalar=par("d_skip", i),
                                       in1=cat[:, 8 + i, NPR:T], op0=ALU.mult, op1=ALU.add).then_inc(y_s_ready, 1)

            dve.wait_ge(xbc_ready, NX // 2 + 1)
            v.tensor_tensor(dtx[:, :, :], xbc[:, 0:KD, NPR:T], chd[:, :, 0:8], ALU.mult).then_inc(dtx_ready, 1)
            difference(0)
            for i in range(2 * NG):
                j = 6 + i // 4
                cuts = [min(8 * (i % 4) + d, KC) for d in (0, 4, 8)]
                if i == NG:
                    dve.wait_ge(st_ready, NG)
                if i + 1 < 2 * NG:
                    difference(i + 1)
                conv(j, cuts[0], cuts[1])
                spread_done(i)
                conv(j, cuts[1], cuts[2])
                take(i)
                if i == 0:
                    dve.wait_ge(out_ssm_s, 16)
                decode_conv(i)
                dve.wait_ge(conv_s_done, i + 1)
                if i >= 2:
                    decode(i - 2)

            def gate_y(gr):
                dve.wait_ge(y_s_ready, 2 * gr + 2)
                v.tensor_tensor(cat[:, 8 + 2 * gr:10 + 2 * gr, :], cat[:, 8 + 2 * gr:10 + 2 * gr, :],
                                zs[:, 2 * gr:2 * gr + 2, :], ALU.mult).then_inc(ycat_ready, 1)

            dve.wait_ge(proj_evac, 2 * NWIN)
            dve.wait_ge(z_ready, 1)
            dve.wait_ge(y_ready, 2 * NG)
            for gr in range(3):
                gate_y(gr)
            decode(6)
            decode(7)
            gate_y(3)
            dve.wait_ge(ln_mean, 1)
            v.tensor_tensor(cat[:, 0:8, :], cat[:, 0:8, :],
                            ps[:, 7, 0:T].unsqueeze(1).to_broadcast([P, KD, T]), ALU.subtract).then_inc(ln_xc, 1)
            for gr in range(NG):
                dve.wait_ge(g_root, gr + 1)
                for j in (2 * gr, 2 * gr + 1):
                    v.scalar_tensor_tensor(out=cat[:, 8 + j, :], in0=cat[:, 8 + j, :], scalar=par("ssm_g", j),
                                           in1=ps[:, 3 + gr, 0:T], op0=ALU.mult, op1=ALU.mult).then_inc(m_out_ready, 1)
            dve.wait_ge(ln_root, 1)
            for j in range(0, KD, 2):
                v.tensor_tensor(cat[:, j:j + 2, :], cat[:, j:j + 2, :],
                                ps[:, 7, 0:T].unsqueeze(1).to_broadcast([P, 2, T]), ALU.mult).then_inc(ln_n, 1)
            for n in range(KD):
                dve.wait_ge(o_psum, n + 1)
                v.tensor_tensor(h[:, n, :], h[:, n, :], ps[:, n, 0:T], ALU.add).then_inc(o_added, 1)
            dve.wait_ge(o_added, KD)
            normed(u, "g_ffn", 2, u_ready)

            dve.wait_ge(consts, 2)
            dve.wait_ge(in_wr, 32)
            dve.wait_ge(log_psum, 1)
            v.tensor_scalar(logit_f, ps[0:20, 7, 0:T], br, None, ALU.add).then_inc(logf_ready, 1)
            dve.wait_ge(logt_psum, 1)
            v.tensor_copy(logit[:, 0:2, :], ps[:, 6, 64:104].rearrange("p (t n) -> p t n", t=2))
            link(v.tensor_copy(logit[0:NSM, 2, :], ps[0:NSM, 6, 104:124]))
            b4 = lambda x: x.to_broadcast([P, 3, 4])
            i4 = iota4.unsqueeze(1).to_broadcast([P, 3, 4])
            link(v.tensor_reduce(gmax, logit[:, :, 0:4], AX.X, ALU.max))
            v.tensor_tensor(gd, logit[:, :, 0:4], b4(gmax), ALU.subtract).then_inc(r_dve, 1)
            dve.wait_ge(r_dve, 1)

            def first_of(d, c, low, onehot):
                link(v.tensor_scalar(c, d, 0.0, -8.0, ALU.is_ge, ALU.mult))
                link(v.tensor_tensor(c, c, i4, ALU.add))
                link(v.tensor_reduce(low, c, AX.X, ALU.min))
                link(v.tensor_tensor(onehot, c, b4(low), ALU.is_equal))

            first_of(gd, gc, gmin, gsel)
            lev = logit[:, :, 4:20].rearrange("p t (g e) -> p t g e", g=4)
            pv = prod16.rearrange("p t (g e) -> p t g e", g=4)
            link(v.tensor_tensor(pv, lev, gsel.unsqueeze(3).to_broadcast([P, 3, 4, 4]), ALU.mult))
            link(v.tensor_reduce(le, pv.rearrange("p t g e -> p t e g"), AX.X, ALU.add))
            link(v.tensor_reduce(m1, le, AX.X, ALU.max))
            link(v.tensor_tensor(ld, le, b4(m1), ALU.subtract))
            first_of(ld, lc, n1, oh1)
            link(v.scalar_tensor_tensor(out=le2, in0=oh1, scalar=-1e30, in1=le, op0=ALU.mult, op1=ALU.add))
            link(v.tensor_reduce(m2, le2, AX.X, ALU.max))
            v.tensor_tensor(t1, m2, m1, ALU.subtract).then_inc(r_dve, 1)
            link(v.tensor_tensor(le2, le2, b4(m2), ALU.subtract))
            first_of(le2, lc2, n2, oh2)
            for o, ohx in ((a1, oh1), (a2, oh2)):
                ins = v.tensor_tensor(o.rearrange("p t (g e) -> p t g e", g=4),
                                      gsel.unsqueeze(3).to_broadcast([P, 3, 4, 4]),
                                      ohx.unsqueeze(2).to_broadcast([P, 3, 4, 4]), ALU.mult)
            link(ins)
            v.tensor_tensor(a12, a1, a2, ALU.add).then_inc(assigned, 1)
            dve.wait_ge(r_act, 1)
            link(v.tensor_reduce(gsum, gexp, AX.X, ALU.add))
            dve.wait_ge(r_act, 2)
            link(v.tensor_scalar(w2, e2, 1.0, None, ALU.add))
            link(v.tensor_tensor(gsum, gsum, w2, ALU.mult))
            link(v.reciprocal(w1, gsum))
            link(v.tensor_tensor(w2, w1, e2, ALU.mult))
            dve.wait_ge(utok_psum, 3)
            v.tensor_copy(utok[0:NSM, 2, :].rearrange("p (b n) -> p b n", b=2), ps[0:NSM, 4:6, :])\
                .then_inc(utok_last, 1)
            dve.wait_ge(pos_psum, 1)
            v.tensor_copy(pos[:, 0:2, :], ps[:, 6, 0:32].rearrange("p (t n) -> p t n", t=2))
            v.tensor_copy(pos[0:NSM, 2, :], ps[0:NSM, 6, 32:48])
            link(v.tensor_copy(tot, ps[:, 6, 48:64]))
            pair = lambda at, n: r0[:, at:at + 6 * n].rearrange("p (x t n) -> p x t n", x=2, t=3)
            a_both, p_both = pair(308, 16), pair(r_pos, 16)
            n_both, q_both, ps_both, gs_both = [pair(60 + 3 * i, 1) for i in (6, 13, 15, 11)]
            link(v.tensor_tensor(p_both, a_both, pos.unsqueeze(1).to_broadcast([P, 2, 3, 16]), ALU.mult))
            link(v.tensor_reduce(ps_both, p_both, AX.X, ALU.add))
            link(v.tensor_scalar(q_both, ps_both, float(CAP), None, ALU.is_ge))
            for r in range(2, MAXQ):
                link(v.scalar_tensor_tensor(out=q_both, in0=ps_both, scalar=float(CAP * r), in1=q_both, op0=ALU.is_ge,
                                            op1=ALU.add))
            link(v.tensor_scalar(gs_both, n_both, float(CAP), float(8 * CAP + 32 * CAP), ALU.mult, ALU.add))
            link(v.scalar_tensor_tensor(out=gs_both, in0=gmin.unsqueeze(1).to_broadcast([P, 2, 3, 1]),
                                        scalar=float(4 * CAP), in1=gs_both, op0=ALU.mult, op1=ALU.add))
            link(v.scalar_tensor_tensor(out=gs_both, in0=q_both, scalar=float(NE * CAP - CAP), in1=gs_both, op0=ALU.mult,
                                        op1=ALU.add))
            link(v.tensor_tensor(gs_both, gs_both, ps_both, ALU.add))

            def make_sel():
                for t in range(3):
                    ins = v.tensor_scalar(sel[:, t, :], iota_s, gs1[:, t, :], None, ALU.is_equal)
                return ins

            def add_sel():
                for t in range(3):
                    ins = v.scalar_tensor_tensor(out=sel[:, t, :], in0=iota_s, scalar=gs2[:, t, :], in1=sel[:, t, :],
                                                 op0=ALU.is_equal, op1=ALU.add)
                return ins

            dve.wait_ge(m_out_ready, KD)
            link(make_sel())
            add_sel().then_inc(sel_ready, 1)
            link(v.tensor_reduce(mc, tot, AX.X, ALU.max))
            link(v.tensor_scalar(nr, mc, float(CAP), None, ALU.is_gt))
            for r in range(2, MAXQ):
                link(v.scalar_tensor_tensor(out=nr, in0=mc, scalar=float(CAP * r), in1=nr, op0=ALU.is_gt, op1=ALU.add))
            v.tensor_scalar(nsteps[:, 0:1], nr, float(PAIRS), float(PAIRS), ALU.mult, ALU.add)
            v.tensor_scalar(nsteps[:, 2:3], nr, 3.0 * PAIRS, 3.0 * PAIRS - 1, ALU.mult, ALU.add)
            v.tensor_scalar(nsteps[:, 1:2], nr, float(PAIRS), float(PAIRS + 1), ALU.mult, ALU.add).then_inc(routes, 1)
            for q in range(3):
                dve.sem_inc(sc_added[q], 1)
            dve.sem_inc(selt_ready, 1)
            dve.wait_ge(routes, 1)
            end = dve.value_load(nsteps[0:1, 1:2], min_val=PAIRS + 1, max_val=PAIRS * MAXQ + 1)
            steps = dve.value_load(nsteps[0:1, 0:1], min_val=PAIRS, max_val=PAIRS * MAXQ)
            with dve.Fori(1, end) as step:
                for t in range(3):
                    v.tensor_scalar(selw[:, t, :], iota_s, gs1[:, t, :], w1[:, t, :], ALU.is_equal, ALU.mult)
                    ins = v.tensor_scalar(seltmp[:, t, :], iota_s, gs2[:, t, :], w2[:, t, :], ALU.is_equal, ALU.mult)
                ins.then_inc(selw_parts, 1)
                dve.wait_ge(selw_parts, step)
                v.tensor_tensor(selw, selw, seltmp, ALU.add).then_inc(selw_ready, 1)
                v.tensor_scalar(gs1, gs1, -2.0 * CAP, None, ALU.add)
                v.tensor_scalar(gs2, gs2, -2.0 * CAP, None, ALU.add).then_inc(gs_moved, 1)
                dve.wait_ge(gs_moved, step)
                dve.wait_ge(xg_psum, step)
                make_sel().then_inc(sel_half, 1)
                dve.wait_ge(sel_half, step)
                add_sel().then_inc(sel_ready, 1)
                dve.wait_ge(silu_ready, step)
                dve.wait_ge(up_done, step)
                v.tensor_tensor(hid, silu_e, ps[:, 1, :], ALU.mult).then_inc(hid_ready, 1)
                dve.wait_ge(selt_psum, step)
                v.tensor_copy(selt, ps[:, 0, 0:T]).then_inc(selt_ready, 1)
                for c in range(KD):
                    q = c % 3
                    dve.wait_ge(sc_psum[q], SC_N[q] * step - SC_N[q] + 1 + c // 3)
                    v.tensor_tensor(h[:, c, :], h[:, c, :], ps[:, SC[q], 0:T], ALU.add).then_inc(sc_added[q], 1)
            for q in range(3):
                dve.wait_ge(sc_added[q], SC_N[q] * steps + 1)
            for k in range(KD):
                v.tensor_scalar(u[:, k, :], h[:, k, :], par("g_ple", k), None, ALU.mult).then_inc(u_ready, 1)
            dve.wait_ge(rs_ready, 3)

            def scale_gate(j):
                dve.wait_ge(gate_psum, j + 1)
                v.tensor_tensor(sg[:, j % 4, :], ps[:, j % 4, 0:T], rs_gate, ALU.mult)\
                    .then_inc(gate_scaled, 1)

            scale_gate(0)
            for j in range(KD):
                dve.wait_ge(gate_sig, j + 1)
                v.tensor_tensor(sg[:, j % 4, :], sg[:, j % 4, :], pw[:, j, :], ALU.mult).then_inc(gate_mul, 1)
                dve.wait_ge(gate_mul, j + 1)
                v.tensor_tensor(h[:, j, :], h[:, j, :], sg[:, j % 4, :], ALU.add).then_inc(h_ple, 1)
                if j + 1 < KD:
                    if j >= 3:
                        dve.wait_ge(h_ple, j - 2)
                    scale_gate(j + 1)
            dve.wait_ge(h_ple, KD)
            normed(yo, "g_final", 4, yo_ready)


def _layout(x):
    f = lambda a: np.asarray(a)

    def feat(a, n):
        a = f(a)
        return np.moveaxis(a.reshape(a.shape[:-1] + (n, P)), (-1, -2), (0, 1))

    def slots(w, k, n):
        w = f(w)
        return w.reshape(k, P, w.shape[1] // n, n).transpose(2, 1, 0, 3).reshape(-1, P, k * n)

    w_in = f(x["w_in"])[0]
    glu_cols = w_in[:, :2 * D].reshape(D, 2, KD, P).transpose(0, 2, 1, 3).reshape(D, KD, 256)
    dt = w_in[:, 5 * D:]
    by_kind = {"g": glu_cols, "z": w_in[:, 2 * D:3 * D].reshape(D, 4, 256), "x": w_in[:, 3 * D:5 * D].reshape(D, 8, 256)}
    gu = [f(x[n])[0].reshape(PAIRS, 2, 2, 4, P, FF).transpose(0, 2, 1, 4, 3, 5) for n in ("w_gate_e", "w_up_e")]
    gu = np.stack(gu, axis=1).reshape(PAIRS, 8, P, SLOT)
    down = f(x["w_down_e"])[0].reshape(PAIRS, 2, 2, 2, P, D).transpose(0, 2, 1, 4, 3, 5).reshape(PAIRS, 4, P, SLOT)
    col = lambda a, n: feat(f(a).reshape(-1), n)
    prm = [col(x["g_mix"], 8), col(x["conf_dw_b"], 8), col(x["conf_ln_g"], 8), col(x["conf_ln_b"], 8),
           col(x["ssm_norm_g"], 8), col(x["g_ffn"], 8), col(x["g_ple"], 8), col(x["g_final"], 8),
           col(np.repeat(f(x["d_skip"])[0], HD), 8), col(x["ssm_conv_b"], 16),
           feat(f(x["conf_dw_w"])[0], 8).reshape(P, -1), feat(f(x["ssm_conv_w"])[0], 16).reshape(P, -1)]
    rows = lambda a, b: np.concatenate([f(a).reshape(NPR, -1), f(b).reshape(NSM, -1)], axis=0)
    ar = {
        "xT": feat(rows(x["x_prompt"], x["x_sample"]), KD),
        "pT": feat(rows(x["p_prompt"], x["p_sample"]), 2),
        "w_in": slots(np.concatenate([by_kind[kind][:, i] for kind, i in W_IN_ORDER], axis=1), KD, 256),
        "w_dt": f(dt).reshape(KD, P, NH).transpose(1, 0, 2),
        "w_out": np.concatenate([slots(f(x["w_out"])[0][half], KD, 256) for half in (slice(D, None), slice(0, D))]),
        "w_moe": np.concatenate([gu, down], axis=1),
        "w_router": np.concatenate([f(x["w_rg"])[0], f(x["w_re"])[0]], axis=1).reshape(KD, P, 20).transpose(1, 0, 2),
        "b_router": np.concatenate([f(x["b_rg"])[0], f(x["b_re"])[0]])[:, None],
        "w_pleg": slots(f(x["w_ple_gate"])[0], KD, 256),
        "w_ple": f(x["w_ple"])[0].reshape(2, P, D),
        "params": np.concatenate(prm, axis=1),
        "hparams": np.stack([f(x["dt_bias"])[0], f(x["a_log"])[0]], axis=1),
        "conf_s": feat(f(x["state_conf_conv"])[0].transpose(1, 0, 2), KD),
        "ssm_s": feat(f(x["state_ssm_conv"])[0].transpose(1, 0, 2), NX),
        "state_s": f(x["state_ssm"])[0].reshape(NSM, KD, P, P).transpose(2, 1, 0, 3),
    }
    return {k: np.ascontiguousarray(v) for k, v in ar.items()}


_OUTS = [("yT", (P, KD, T)), ("conf_p_out", (P, KD, KC - 1)), ("ssm_p_out", (P, NX, KS - 1)), ("h_p_out", (P, D)),
         ("conf_s_out", (P, KD, KC - 1, NSM)), ("ssm_s_out", (P, NX, KS - 1, NSM)), ("h_s_out", (P, KD, NSM, P))]


def kernel(**inputs):
    import concourse.bacc as _bacc
    from concourse.bass_utils import run_bass_kernel_spmd as _run

    nc = _bacc.Bacc("TRN2", target_bir_lowering=False, num_devices=1)
    arrays, args = {}, {}
    for name, a in _layout(inputs).items():
        arrays[f"in_{name}"] = a
        args[name] = nc.dram_tensor(f"in_{name}", a.shape, F32, kind="ExternalInput").ap()
    for name, shape in _OUTS:
        args[name] = nc.dram_tensor(f"out_{name}", shape, F32, kind="ExternalOutput").ap()
    build(nc, **args)
    r = _run(nc, [arrays], core_ids=[0]).results[0]
    o = {name: np.asarray(r[f"out_{name}"]) for name, _ in _OUTS}
    y = o["yT"].transpose(2, 1, 0).reshape(T, D)
    return (
        y[:NPR].reshape(1, NPR, D),
        y[NPR:].reshape(NSM, 1, D),
        o["conf_p_out"].transpose(2, 1, 0).reshape(1, 1, KC - 1, D),
        o["ssm_p_out"].transpose(2, 1, 0).reshape(1, 1, KS - 1, NX * P),
        o["h_p_out"].reshape(P, NH, HD).transpose(1, 2, 0).reshape(1, 1, NH, HD, P),
        o["conf_s_out"].transpose(3, 2, 1, 0).reshape(1, NSM, KC - 1, D),
        o["ssm_s_out"].transpose(3, 2, 1, 0).reshape(1, NSM, KS - 1, NX * P),
        o["h_s_out"].transpose(2, 1, 0, 3).reshape(1, NSM, NH, HD, P),
    )
```
